# Optimizing a Trainium2 kernel written in Bass

```python
import jax, jax.numpy as jnp
from jax import lax
import numpy as np

D_MODEL = 1024
BATCH = 1
SEQ = 1024
DEPTH = 2

GRID_W = 64
CTX_LEN = 256
Q_BLOCK = 128
ROPE_BASE = 10000.0
RMS_EPS = 1e-6
LN_EPS = 1e-5

MLA_HEADS = 8
MLA_Q_LORA = 384
MLA_KV_LORA = 256
MLA_NOPE = 64
MLA_ROPE = 32
MLA_V = 64
MLA_QK = MLA_NOPE + MLA_ROPE
MLA_SCALE = MLA_QK ** -0.5

HEAD_DIM = 64
GQA_HEADS = 8
GQA_KV_HEADS = 2
GQA_GROUP = GQA_HEADS // GQA_KV_HEADS
GQA_SCALE = HEAD_DIM ** -0.5

MIX_WIDTH = MLA_HEADS * MLA_V + GQA_HEADS * HEAD_DIM
IN_SPLITS = (MLA_Q_LORA,
             MLA_Q_LORA + MLA_KV_LORA,
             MLA_Q_LORA + MLA_KV_LORA + MLA_ROPE,
             MLA_Q_LORA + MLA_KV_LORA + MLA_ROPE + GQA_HEADS * HEAD_DIM,
             MLA_Q_LORA + MLA_KV_LORA + MLA_ROPE + (GQA_HEADS + GQA_KV_HEADS) * HEAD_DIM)
IN_COLS = MLA_Q_LORA + MLA_KV_LORA + MLA_ROPE + (GQA_HEADS + 2 * GQA_KV_HEADS) * HEAD_DIM

N_GROUPS = 4
EXPERTS_PER_GROUP = 8
N_EXPERTS = N_GROUPS * EXPERTS_PER_GROUP
TOP_K = 2
D_FF_EXPERT = 512
MOE_BLOCK = 128

ALPHA = (2.0 * DEPTH) ** 0.25
BETA = (8.0 * DEPTH) ** -0.25

kernel_name = "hybrid_mla_gqa_hmoe_diffusion_block"

def rms_norm(x, g):
    xf = x.astype(jnp.float32)
    y = xf * lax.rsqrt(jnp.mean(jnp.square(xf), axis=-1, keepdims=True) + RMS_EPS)
    return (y * g).astype(x.dtype)

def layer_norm(x, g, b):
    xf = x.astype(jnp.float32)
    mu = jnp.mean(xf, axis=-1, keepdims=True)
    var = jnp.mean(jnp.square(xf - mu), axis=-1, keepdims=True)
    return ((xf - mu) * lax.rsqrt(var + LN_EPS) * g + b).astype(x.dtype)

def modulate(x, shift, scale):
    return x * (1 + scale) + shift

def rope_1d(x, ang):
    d2 = ang.shape[-1]
    cos = jnp.cos(ang)[:, None, :]
    sin = jnp.sin(ang)[:, None, :]
    xf = x.astype(jnp.float32)
    x1, x2 = xf[..., :d2], xf[..., d2:]
    return jnp.concatenate([x1 * cos - x2 * sin, x2 * cos + x1 * sin], axis=-1).astype(x.dtype)

def rope_2d(x, row, col):
    half = x.shape[-1] // 2
    inv = ROPE_BASE ** (-(jnp.arange(0, half, 2, dtype=jnp.float32) / half))
    return jnp.concatenate([rope_1d(x[..., :half], row[:, None] * inv),
                            rope_1d(x[..., half:], col[:, None] * inv)], axis=-1)

def blocked_attention(q, k, v, scale):
    B, L, Hk, G, Dq = q.shape
    nb = L // Q_BLOCK
    qb = jnp.moveaxis(q.reshape(B, nb, Q_BLOCK, Hk, G, Dq), 1, 0)

    def one_block(qblk):
        s = jnp.einsum('bqhgd,bkhd->bhgqk', qblk, k, preferred_element_type=jnp.float32) * scale
        p = jax.nn.softmax(s, axis=-1)
        return jnp.einsum('bhgqk,bkhd->bqhgd', p.astype(v.dtype), v)

    o = lax.map(one_block, qb)
    return jnp.moveaxis(o, 0, 1).reshape(B, L, Hk * G * v.shape[-1])

def mixer_inputs(h, p_attn, row, col):
    w_in, g_q_a, w_q_b, g_kv_a, w_kv_b, g_gq, g_gk = p_attn
    B, L, _ = h.shape
    z = h @ w_in
    q_a, kv_a, k_rope, gq, gk, gv = jnp.split(z, IN_SPLITS, axis=-1)
    q = (rms_norm(q_a, g_q_a) @ w_q_b).reshape(B, L, MLA_HEADS, MLA_QK)
    q_nope, q_rope = q[..., :MLA_NOPE], q[..., MLA_NOPE:]
    kv = (rms_norm(kv_a, g_kv_a) @ w_kv_b).reshape(B, L, MLA_HEADS, MLA_NOPE + MLA_V)
    k_nope, v_mla = kv[..., :MLA_NOPE], kv[..., MLA_NOPE:]
    k_rope = k_rope.reshape(B, L, 1, MLA_ROPE)
    gq = rms_norm(gq.reshape(B, L, GQA_HEADS, HEAD_DIM), g_gq)
    gk = rms_norm(gk.reshape(B, L, GQA_KV_HEADS, HEAD_DIM), g_gk)
    gv = gv.reshape(B, L, GQA_KV_HEADS, HEAD_DIM)
    if row is not None:
        q_rope = rope_2d(q_rope, row, col)
        k_rope = rope_2d(k_rope, row, col)
        gq = rope_2d(gq, row, col)
        gk = rope_2d(gk, row, col)
    q_mla = jnp.concatenate([q_nope, q_rope], axis=-1)[:, :, :, None, :]
    k_mla = jnp.concatenate([k_nope, jnp.broadcast_to(k_rope, (B, L, MLA_HEADS, MLA_ROPE))], axis=-1)
    q_gqa = gq.reshape(B, L, GQA_KV_HEADS, GQA_GROUP, HEAD_DIM)
    return q_mla, k_mla, v_mla, q_gqa, gk, gv

def moe_ffn(h, w_grp, b_grp, w_exp, b_exp, w_gate, w_up, w_down):
    T, D = h.shape
    lg = (h @ w_grp + b_grp).astype(jnp.float32)
    pg = jax.nn.softmax(lg, axis=-1)
    g_star = jnp.argmax(lg, axis=-1)
    p_star = jnp.take_along_axis(pg, g_star[:, None], axis=-1)
    le = (h @ w_exp + b_exp).astype(jnp.float32).reshape(T, N_GROUPS, EXPERTS_PER_GROUP)
    le_g = jnp.take_along_axis(le, g_star[:, None, None], axis=1)[:, 0]
    top_v, top_i = lax.top_k(le_g, TOP_K)
    weights = (p_star * jax.nn.softmax(top_v, axis=-1)).astype(h.dtype)
    expert_id = g_star[:, None] * EXPERTS_PER_GROUP + top_i

    A = T * TOP_K
    flat_e = expert_id.reshape(A)
    order = jnp.argsort(flat_e)
    sorted_e = flat_e[order]
    counts = jnp.bincount(flat_e, length=N_EXPERTS)
    padded = (counts + MOE_BLOCK - 1) // MOE_BLOCK * MOE_BLOCK
    pad_end = jnp.cumsum(padded)
    pad_start = pad_end - padded
    start = jnp.cumsum(counts) - counts
    dest_sorted = pad_start[sorted_e] + jnp.arange(A) - start[sorted_e]
    n_blocks = -(-A // MOE_BLOCK) + N_EXPERTS
    slot_tok = jnp.zeros((n_blocks * MOE_BLOCK,), jnp.int32).at[dest_sorted].set(order // TOP_K)
    block_e = jnp.minimum(jnp.searchsorted(pad_end, jnp.arange(n_blocks) * MOE_BLOCK, side='right'),
                          N_EXPERTS - 1)
    xb = h[slot_tok].reshape(n_blocks, MOE_BLOCK, D)

    def expert_block(args):
        xblk, e = args
        return (jax.nn.silu(xblk @ w_gate[e]) * (xblk @ w_up[e])) @ w_down[e]

    yb = lax.map(expert_block, (xb, block_e)).reshape(n_blocks * MOE_BLOCK, D)
    dest = jnp.zeros((A,), jnp.int32).at[order].set(dest_sorted)
    y = yb[dest].reshape(T, TOP_K, D)
    return jnp.einsum('tk,tkd->td', weights, y)

def setup_inputs(seed: int = 0) -> dict:
    key = jax.random.key(seed)
    ks = jax.random.split(key, 26)
    f32 = jnp.float32
    L, D = DEPTH, D_MODEL

    def nrm(k, shape, scale):
        return jax.random.normal(k, shape, f32) * scale

    return {
        "x": nrm(ks[0], (BATCH, SEQ, D), 1.0),
        "c": nrm(ks[1], (BATCH, D), 1.0),
        "ctx": nrm(ks[2], (BATCH, CTX_LEN, D), 1.0),
        "c_ctx": nrm(ks[3], (D,), 1.0),
        "w_ada": nrm(ks[4], (L, D, 6 * D), D ** -0.5),
        "b_ada": nrm(ks[5], (L, 6 * D), 0.02),
        "w_in": nrm(ks[6], (L, D, IN_COLS), D ** -0.5),
        "g_q_a": 1.0 + nrm(ks[7], (L, MLA_Q_LORA), 0.02),
        "w_q_b": nrm(ks[8], (L, MLA_Q_LORA, MLA_HEADS * MLA_QK), MLA_Q_LORA ** -0.5),
        "g_kv_a": 1.0 + nrm(ks[9], (L, MLA_KV_LORA), 0.02),
        "w_kv_b": nrm(ks[10], (L, MLA_KV_LORA, MLA_HEADS * (MLA_NOPE + MLA_V)), MLA_KV_LORA ** -0.5),
        "g_gqa_q": 1.0 + nrm(ks[11], (L, HEAD_DIM), 0.02),
        "g_gqa_k": 1.0 + nrm(ks[12], (L, HEAD_DIM), 0.02),
        "w_o": nrm(ks[13], (L, MIX_WIDTH, D), MIX_WIDTH ** -0.5 * BETA),
        "ln1_g": 1.0 + nrm(ks[14], (L, D), 0.02),
        "ln1_b": nrm(ks[15], (L, D), 0.02),
        "w_router_grp": nrm(ks[16], (L, D, N_GROUPS), D ** -0.5),
        "b_router_grp": nrm(ks[17], (L, N_GROUPS), 0.01),
        "w_router_exp": nrm(ks[18], (L, D, N_EXPERTS), D ** -0.5),
        "b_router_exp": nrm(ks[19], (L, N_EXPERTS), 0.01),
        "w_gate": nrm(ks[20], (L, N_EXPERTS, D, D_FF_EXPERT), D ** -0.5),
        "w_up": nrm(ks[21], (L, N_EXPERTS, D, D_FF_EXPERT), D ** -0.5),
        "w_down": nrm(ks[22], (L, N_EXPERTS, D_FF_EXPERT, D), D_FF_EXPERT ** -0.5 * BETA),
        "ln2_g": 1.0 + nrm(ks[23], (L, D), 0.02),
        "ln2_b": nrm(ks[24], (L, D), 0.02),
    }

def reference(x, c, ctx, c_ctx, w_ada, b_ada, w_in, g_q_a, w_q_b, g_kv_a, w_kv_b, g_gqa_q, g_gqa_k,
              w_o, ln1_g, ln1_b, w_router_grp, b_router_grp, w_router_exp, b_router_exp,
              w_gate, w_up, w_down, ln2_g, ln2_b):
    B, S, D = x.shape
    C = ctx.shape[1]
    rows = S // GRID_W
    row = jnp.repeat(jnp.arange(rows, dtype=jnp.float32), GRID_W)
    col = jnp.tile(jnp.arange(GRID_W, dtype=jnp.float32), rows)
    silu_c = jax.nn.silu(c)
    silu_cc = jax.nn.silu(c_ctx)
    xc = ctx
    for l in range(DEPTH):
        last = l == DEPTH - 1
        sh_a, sc_a, ga, sh_f, sc_f, gf = jnp.split((silu_c @ w_ada[l] + b_ada[l])[:, None, :], 6, axis=-1)
        csh_a, csc_a, cga, csh_f, csc_f, cgf = jnp.split(silu_cc @ w_ada[l] + b_ada[l], 6, axis=-1)
        p_attn = (w_in[l], g_q_a[l], w_q_b[l], g_kv_a[l], w_kv_b[l], g_gqa_q[l], g_gqa_k[l])

        qm, km, vm, qg, kg, vg = mixer_inputs(modulate(x, sh_a, sc_a), p_attn, row, col)
        qmc, kmc, vmc, qgc, kgc, vgc = mixer_inputs(modulate(xc, csh_a, csc_a), p_attn, None, None)
        o = jnp.concatenate([
            blocked_attention(qm, jnp.concatenate([kmc, km], axis=1),
                              jnp.concatenate([vmc, vm], axis=1), MLA_SCALE),
            blocked_attention(qg, jnp.concatenate([kgc, kg], axis=1),
                              jnp.concatenate([vgc, vg], axis=1), GQA_SCALE)], axis=-1)
        x = layer_norm(ALPHA * x + ga * (o @ w_o[l]), ln1_g[l], ln1_b[l])
        if not last:
            oc = jnp.concatenate([blocked_attention(qmc, kmc, vmc, MLA_SCALE),
                                  blocked_attention(qgc, kgc, vgc, GQA_SCALE)], axis=-1)
            xc = layer_norm(ALPHA * xc + cga * (oc @ w_o[l]), ln1_g[l], ln1_b[l])

        p_moe = (w_router_grp[l], b_router_grp[l], w_router_exp[l], b_router_exp[l],
                 w_gate[l], w_up[l], w_down[l])
        h = modulate(x, sh_f, sc_f).reshape(B * S, D)
        if last:
            y = moe_ffn(h, *p_moe).reshape(B, S, D)
        else:
            hc = modulate(xc, csh_f, csc_f).reshape(B * C, D)
            y_all = moe_ffn(jnp.concatenate([h, hc], axis=0), *p_moe)
            y = y_all[:B * S].reshape(B, S, D)
            xc = layer_norm(ALPHA * xc + cgf * y_all[B * S:].reshape(B, C, D), ln2_g[l], ln2_b[l])
        x = layer_norm(ALPHA * x + gf * y, ln2_g[l], ln2_b[l])
    return x


_drawn_inputs = setup_inputs


def setup_inputs(seed=0):
    import zlib

    import numpy as np

    out = dict(_drawn_inputs(seed))
    spreads = {}
    factors = {'ctx': 4.284,
     'g_q_a': 8.0,
     'g_kv_a': 8.0,
     'g_gqa_q': 8.0,
     'g_gqa_k': 8.0,
     'b_router_grp': 8.0,
     'b_router_exp': 6.266}
    for name, (base, spread) in spreads.items():
        noise = np.random.default_rng([zlib.crc32(name.encode()), seed]).standard_normal(out[name].shape)
        drawn = base * np.exp(spread * noise) if base else spread * noise
        out[name] = __import__('jax').numpy.asarray(drawn.astype(out[name].dtype))
    for name, factor in factors.items():
        out[name] = (out[name] * factor).astype(out[name].dtype)
    return out
```

```python
import numpy as np
import concourse.bass as bass
from concourse import mybir
from contextlib import ExitStack, contextmanager

F32 = mybir.dt.float32
I32 = mybir.dt.int32
F32R = mybir.dt.float32r
ALU = mybir.AluOpType
ACT = mybir.ActivationFunctionType
AX = mybir.AxisListType

P = 128
D = 1024
SEQ = 1024
CTX = 256
DEPTH = 2
KC = D // P
CT = CTX // P
LT = SEQ // P
NT = CT + LT
GRID_W = 64
ROPE_BASE = 10000.0
RMS_EPS = 1e-6
LN_EPS = 1e-5
H_MLA, QLORA, KVLORA, NOPE, ROPE, VD = 8, 384, 256, 64, 32, 64
QK = NOPE + ROPE
MLA_SCALE = QK ** -0.5
H_GQA, H_KV, HD = 8, 2, 64
GQA_SCALE = HD ** -0.5
HEADS = H_MLA + H_GQA
Z_KR = QLORA + KVLORA
Z_G = Z_KR + ROPE
G_ALL = H_GQA + H_KV
Z_V = Z_G + G_ALL * HD
Z_ALL = Z_V + H_KV * HD
NGRP, PER, NE, TOPK, FF = 4, 8, 32, 2, 512
ALPHA = (2.0 * DEPTH) ** 0.25
BIG = 1.0e30


def n_blocks(tiles):
    return (tiles * P * TOPK + NE * (P - 1)) // P


NB = n_blocks(NT)
NBP = NB + NB % 2


class Chain:

    def __init__(self, eng, sem):
        self.eng, self.sem, self.base, self.n = eng, sem, 0, 0

    def start(self, base):
        self.base, self.n = base, 0

    def step(self, ins):
        ins.then_inc(self.sem, 1)
        self.n += 1
        return self.base + self.n

    def link(self, ins):
        self.eng.wait_ge(self.sem, self.step(ins))


@contextmanager
def semaphores(nc):
    got = []

    def new(name):
        got.append(nc.alloc_semaphore(name))
        return got[-1]

    yield new
    nc.clear_and_free_semaphores(got)
    nc.all_engine_barrier()



def modulation(nc, A, S):
    NW, BUF = 512, 3
    with ExitStack() as cx:
        new_semaphore = cx.enter_context(semaphores(nc))
        wt = cx.enter_context(nc.sbuf_tensor("ada_w", [P, BUF, KC, NW], F32))
        ccol = cx.enter_context(nc.sbuf_tensor("ada_c", [P, 2, KC], F32))
        scol = cx.enter_context(nc.sbuf_tensor("ada_silu", [P, KC, 2], F32))
        brow = cx.enter_context(nc.sbuf_tensor("ada_bias", [2, DEPTH * 6 * D], F32))
        row = cx.enter_context(nc.sbuf_tensor("ada_row", [2, DEPTH * 6 * D], F32))
        ps = cx.enter_context(nc.psum_tensor("ada_ps", [P, BUF, NW], F32))
        w_full = [new_semaphore(f"ada_w_full{u}") for u in range(BUF)]
        small = new_semaphore("ada_small_loaded")
        silu_done = new_semaphore("ada_silu_done")
        mm_done = new_semaphore("ada_mm_done")
        evac = new_semaphore("ada_evacuated")
        stored = new_semaphore("ada_stored")
        copied = new_semaphore("stream_copied")
        per = 6 * D // NW // BUF
        block = cx.enter_context(nc.Block())

        @block.sync
        def _(sp):
            for layer in range(DEPTH):
                w = A["w_ada"][layer].rearrange("(p a) n -> p a n", a=KC)
                with sp.Fori(0, per) as i:
                    for u in range(BUF):
                        if layer:
                            sp.wait_ge(mm_done, (i + layer * per - 1) * BUF + u + 1)
                            sp.dma_start(wt[:, u], w[:, :, bass.ds((i * BUF + u) * NW, NW)]).then_inc(w_full[u], 16)
                        else:
                            sp.wait_ge(mm_done, i * BUF)
                            sp.dma_start(wt[:, u], w[:, :, bass.ds((i * BUF + u) * NW, NW)]).then_inc(w_full[u], 16)
            sp.wait_ge(evac, DEPTH * per * BUF)
            sp.dma_start(S["ada"][:, :], row[:, :]).then_inc(stored, 16)
            sp.wait_ge(stored, 16)

        @block.scalar
        def _(act):
            act.dma_start(ccol[:, 0, :], A["c_ctx"].rearrange("(p a) -> p a", a=KC)).then_inc(small, 16)
            act.dma_start(ccol[:, 1, :], A["c"][0].rearrange("(p a) -> p a", a=KC)).then_inc(small, 16)
            act.dma_start(brow[:, :], A["b_ada"].rearrange("l n -> (l n)").partition_broadcast(2)).then_inc(small, 16)
            act.dma_start(S["x_s"][0:CTX, :], A["ctx"][0]).then_inc(copied, 16)
            act.dma_start(S["x_s"][CTX:CTX + SEQ, :], A["x"][0]).then_inc(copied, 16)
            act.wait_ge(small, 48)
            nc.scalar.activation(scol[:, :, :].rearrange("p a s -> p s a"), ccol[:, :, :], ACT.Silu).then_inc(silu_done, 1)
            act.wait_ge(copied, 32)

        @block.tensor
        def _(pe):
            pe.wait_ge(silu_done, 1)
            for layer in range(DEPTH):
                with pe.Fori(0, per) as i:
                    for u in range(BUF):
                        pe.wait_ge(w_full[u], (i + layer * per + 1) * 16)
                        if layer:
                            pe.wait_ge(evac, (i + layer * per - 1) * BUF + u + 1)
                        else:
                            pe.wait_ge(evac, i * BUF)
                        for k in range(KC):
                            last = nc.tensor.matmul(ps[0:2, u, :], scol[:, k, :], wt[:, u, k, :],
                                                    start=(k == 0), stop=(k == KC - 1))
                        last.then_inc(mm_done, 1)

        @block.vector
        def _(dve):
            dve.wait_ge(small, 48)
            for layer in range(DEPTH):
                with dve.Fori(0, per) as i:
                    for u in range(BUF):
                        dve.wait_ge(mm_done, (i + layer * per) * BUF + u + 1)
                        cols = bass.ds((i * BUF + u) * NW + layer * 6 * D, NW)
                        nc.vector.tensor_tensor(row[:, cols], ps[0:2, u, :], brow[:, cols], ALU.add).then_inc(evac, 1)



def projections(nc, A, S, C, layer):
    last_layer = layer == DEPTH - 1
    ZW = Z_ALL // 3
    with ExitStack() as cx:
        new_semaphore = cx.enter_context(semaphores(nc))

        def sb(name, shape, dt=F32):
            return cx.enter_context(nc.sbuf_tensor(f"{name}{layer}", shape, dt))

        def sem(name):
            return new_semaphore(f"{name}{layer}")

        w_in = sb("w_in", [P, KC, Z_ALL])
        w_q = sb("w_q", [P, QLORA // P, H_MLA * QK])
        w_kv = sb("w_kv", [P, KVLORA // P, H_MLA * (NOPE + VD)])
        g_col = sb("g_col", [P, 5])
        g_row = sb("g_row", [P, G_ALL, HD])
        mod = sb("mod", [P, 2, 2, KC])
        modt = sb("modt", [P, NT, 2, KC])
        xt = sb("xt", [P, D])
        hT = sb("hT", [P, KC, P])
        z = sb("z", [P, Z_ALL])
        junk = sb("junk", [P, QLORA])
        sq = sb("sq", [P, G_ALL, HD])
        ms = sb("ms", [P, 2 + G_ALL])
        rstd = sb("rstd", [P, 2 + G_ALL])
        qa = sb("qa", [P, 5, P])
        qaT = sb("qaT", [P, 5, P])
        q_tok = sb("q_tok", [P, H_MLA + 1, QK])
        k_tok = sb("k_tok", [P, H_MLA, QK])
        gn = sb("gn", [P, G_ALL, HD])
        vg = sb("vg", [P, H_KV * HD])
        g_tok = sb("g_tok", [P, G_ALL, HD])
        r_a = sb("r_a", [P, G_ALL, HD])
        r_b = sb("r_b", [P, G_ALL, HD])
        gq2 = sb("gq2", [P, H_GQA, 2, HD], F32R)
        gk2 = sb("gk2", [P, 2, H_KV, 2, HD], F32R)
        qT = [sb(f"qT{n}", [QK, H_MLA, P], F32R) for n in range(2)]
        kT = [sb(f"kT{n}", [QK, H_MLA, P], F32R) for n in range(2)]
        gqT = sb("gqT", [P, H_GQA, P], F32R)
        gkT = sb("gkT", [P, 2 * H_KV, P], F32R)
        v = sb("v", [P, (H_MLA + H_KV) * VD])
        rope_mla = sb("rope_mla", [P, NT, 2, ROPE])
        rope_gqa = sb("rope_gqa", [P, NT, 2, HD])
        tp = [cx.enter_context(nc.psum_tensor(f"tp{b}_{layer}", [P, 4, P], F32)) for b in range(2)]
        zp = cx.enter_context(nc.psum_tensor(f"zp{layer}", [P, 3, 512], F32))
        up = cx.enter_context(nc.psum_tensor(f"up{layer}", [P, 3, 512], F32))

        w_loaded, x_loaded = sem("w_loaded"), sem("x_loaded")
        prep = sem("prep")
        t_full, freed, hi_done = sem("t_full"), [sem("freed0"), sem("freed1")], sem("hi_done")
        z_full, z_out = sem("z_full"), sem("z_out")
        z_act, norm_in, norm_out, qa_ready = sem("z_act"), sem("norm_in"), sem("norm_out"), sem("qa_ready")
        up_full, up_act, up_dve = sem("up_full"), sem("up_act"), sem("up_dve")
        modt_ready, q_stored, eps_added = sem("modt_ready"), sem("q_stored"), sem("eps_added")
        g_hi, t_loaded = sem("g_hi"), sem("t_loaded")
        dve_step, act_step, pool_step = sem("dve_step"), sem("act_step"), sem("pool_step")
        block = cx.enter_context(nc.Block())

        PRE, A2, B1 = 8, 5, 16
        TG = 12
        NST = 7

        @block.sync
        def _(sp):
            def load_x(t):
                sp.dma_start(xt[:, :], S["x_s"].rearrange("(t p) n -> t p n", p=P)[bass.ds(t, 1)]
                             .rearrange("a p n -> p (a n)")).then_inc(x_loaded, 16)

            def store(t, ends=0):
                for b in range(2):
                    sp.wait_ge(freed[b], 1 + 6 * t + 6 - ends)
                for n in range(2):
                    sp.dma_start(S["q_mla"][bass.ds(t, 1), n].rearrange("a p h n -> p (a h) n"),
                                 qT[n][:, :, :].bitcast(F32)).then_inc(q_stored, 16)
                    sp.dma_start(S["k_mla"][n, :, :, bass.ds(t * P, P)], kT[n][:, :, :].bitcast(F32)).then_inc(q_stored, 16)
                sp.dma_start(S["q_gqa"][bass.ds(t, 1)].rearrange("a p h n -> p (a h) n"), gqT[:, :, :].bitcast(F32)).then_inc(q_stored, 16)
                sp.dma_start(S["k_gqa"][:, :, bass.ds(t * P, P)], gkT[:, :, :].bitcast(F32)).then_inc(q_stored, 16)
                sp.dma_start(S["v_s"].rearrange("(t p) n -> t p n", p=P)[bass.ds(t, 1)]
                             .rearrange("a p n -> p (a n)"), v[:, :]).then_inc(q_stored, 16)

            w = A["w_in"][layer].rearrange("(a p) n -> p a n", p=P)
            load_x(0)
            sp.dma_start(rope_mla[:, :, :, :], C["dram"]["rope_mla"]).then_inc(t_loaded, 16)
            sp.dma_start(rope_gqa[:, :, :, :], C["dram"]["rope_gqa"]).then_inc(t_loaded, 16)
            sp.dma_start(w_in[:, :, :], w).then_inc(w_loaded, 16)
            sp.dma_start(w_q[:, :, :], A["w_q_b"][layer].rearrange("(a p) n -> p a n", p=P)).then_inc(w_loaded, 16)
            sp.dma_start(w_kv[:, :, :], A["w_kv_b"][layer].rearrange("(a p) n -> p a n", p=P)).then_inc(w_loaded, 16)
            sp.wait_ge(t_full, 2)
            load_x(1)
            store(0)
            with sp.Fori(2, NT) as t:
                sp.wait_ge(t_full, 2 + TG * (t - 2) + 2)
                load_x(t)
                store(t - 1)
            store(NT - 1, 1)
            sp.wait_ge(q_stored, 16 * NST * NT)

        @block.gpsimd
        def _(pool):
            with nc.allow_non_contiguous_dma(reason="a few thousand column entries"):
                for s in range(2):
                    for n, part in enumerate((0, 1)):
                        o = layer * 6 * D + part * D
                        pool.dma_start(mod[:, s, n, :], S["ada"][s, o:o + D].rearrange("(a p) -> p a", p=P)).then_inc(prep, 16)
                pool.dma_start(g_col[:, 0:3], A["g_q_a"][layer].rearrange("(a p) -> p a", p=P)).then_inc(prep, 16)
                pool.dma_start(g_col[:, 3:5], A["g_kv_a"][layer].rearrange("(a p) -> p a", p=P)).then_inc(prep, 16)
            pool.dma_start(r_a[:, 0, :], A["g_gqa_q"][layer].partition_broadcast(P)).then_inc(prep, 16)
            pool.dma_start(r_a[:, 1, :], A["g_gqa_k"][layer].partition_broadcast(P)).then_inc(prep, 16)
            if layer == 0:
                nc.gpsimd.memset(C["zeros"][:, :], 0.0).then_inc(pool_step, 1)
                pool.wait_ge(pool_step, 1)
                pool.dma_start(S["xb"].rearrange("(b p) n -> p b n", p=P),
                               C["zeros"][:, :].unsqueeze(1).to_broadcast([P, NBP + 2, D])).then_inc(C["xb_zeroed"], 16)
            with pool.Fori(0, NT) as t:
                pool.wait_ge(norm_in, t + 1)
                pool.wait_ge(act_step, 2 * t + 2)
                nc.gpsimd.tensor_tensor(ms[:, :], ms[:, :], C["eps"][:, 0:2 + G_ALL], ALU.add).then_inc(eps_added, 1)
                pool.wait_ge(eps_added, t + 1)
                nc.gpsimd.tensor_tensor(rstd[:, :], ms[:, :], C["mhalf"][:, 0:2 + G_ALL], ALU.pow).then_inc(norm_out, 1)
            if layer == 0:
                pool.wait_ge(C["xb_zeroed"], 16)

        @block.scalar
        def _(act):
            def part_a1(t, g):
                act.wait_ge(t_full, g + 1)
                act.wait_ge(z_full, 3 * t)
                for k in range(4):
                    ins = nc.scalar.activation(hT[:, k, :], tp[0][:, k, :], ACT.Identity,
                                               bias=modt[:, bass.ds(t, 1), 0, k:k + 1].rearrange("p a b -> p (a b)"),
                                               scale=modt[:, bass.ds(t, 1), 1, k:k + 1].rearrange("p a b -> p (a b)"))
                ins.then_inc(freed[0], 1)

            def part_a2(t):
                act.wait_ge(z_full, 3 * t + 1)
                nc.scalar.activation(z[:, 0:ZW], zp[:, 0, 0:ZW], ACT.Copy).then_inc(z_act, 1)
                act.wait_ge(z_act, t + 1)
                act.wait_ge(z_out, 2 * t + 1)
                nc.scalar.activation(junk[:, 0:QLORA], z[:, 0:QLORA], ACT.Square, scale=QLORA ** -0.5,
                                     accum_out=ms[:, 0:1]).then_inc(act_step, 1)
                act.wait_ge(act_step, 2 * t + 1)
                nc.scalar.activation(junk[:, 0:KVLORA], z[:, QLORA:Z_KR], ACT.Square, scale=KVLORA ** -0.5,
                                     accum_out=ms[:, 1:2]).then_inc(act_step, 1)
                act.wait_ge(norm_out, t + 1)
                nc.scalar.activation(qa[:, 0:3, :].rearrange("p a n -> p (a n)"), z[:, 0:QLORA], ACT.Copy,
                                     scale=rstd[:, 0:1])
                nc.scalar.activation(qa[:, 3:5, :].rearrange("p a n -> p (a n)"), z[:, QLORA:Z_KR], ACT.Copy,
                                     scale=rstd[:, 1:2]).then_inc(qa_ready, 1)

            def part_b1(t, g):
                act.wait_ge(t_full, g + 3)
                act.wait_ge(up_full, 4 * t)
                nc.scalar.activation(qaT[:, 0:3, :], tp[0][:, 0:3, :], ACT.Copy).then_inc(freed[0], 1)
                for n in range(2):
                    act.wait_ge(up_full, 4 * t + n + 1)
                    nc.scalar.activation(q_tok[:, 4 * n:4 * n + 4, :], up[:, n, 0:4 * QK].rearrange("p (h d) -> p h d", h=4),
                                         ACT.Copy, scale=MLA_SCALE).then_inc(up_act, 1)
                act.wait_ge(up_full, 4 * t + 3)
                kv = up[:, 2, :].rearrange("p (h d) -> p h d", h=4)
                nc.scalar.activation(k_tok[:, 0:4, 0:NOPE], kv[:, :, 0:NOPE], ACT.Copy)
                act.wait_ge(q_stored, 16 * NST * t)
                nc.scalar.activation(v[:, 0:4 * VD].rearrange("p (h d) -> p h d", h=4),
                                     kv[:, :, NOPE:NOPE + VD], ACT.Copy).then_inc(up_act, 1)
                act.wait_ge(dve_step, PRE + A2 + 6 + t * (A2 + B1))
                nc.scalar.activation(gq2[:, :, 0, :], g_tok[:, 0:H_GQA, :], ACT.Copy)
                nc.scalar.activation(gk2[:, 0, :, :, :], g_tok[:, H_GQA:G_ALL, :].unsqueeze(2).to_broadcast([P, H_KV, 2, HD]),
                                     ACT.Copy).then_inc(g_hi, 1)

            def part_b2(t, g):
                act.wait_ge(q_stored, 16 * NST * t)
                for n, dst in enumerate((kT, kT, qT, qT)):
                    act.wait_ge(t_full, g + 5 + n)
                    h0 = 4 * (n % 2)
                    nc.scalar.activation(dst[0][:, h0:h0 + 4, :], tp[n % 2][0:QK, :, :], ACT.Copy).then_inc(hi_done, 1)
                act.wait_ge(t_full, g + 9)
                nc.scalar.activation(gqT[:, 0:4, :], tp[0][:, :, :], ACT.Copy).then_inc(freed[0], 1)
                act.wait_ge(t_full, g + 11)
                nc.scalar.activation(gkT[:, 0:2, :], tp[0][:, 0:2, :], ACT.Copy).then_inc(freed[0], 1)

            act.wait_ge(prep, 128)
            nc.scalar.activation(modt[:, 0:CT], mod[:, 0:1].to_broadcast([P, CT, 2, KC]), ACT.Copy)
            nc.scalar.activation(modt[:, CT:NT], mod[:, 1:2].to_broadcast([P, LT, 2, KC]), ACT.Copy).then_inc(modt_ready, 1)
            act.wait_ge(dve_step, PRE)
            part_a1(0, 0)
            with act.Fori(1, NT) as t:
                g = 2 + TG * (t - 1)
                part_a1(t, g)
                part_a2(t - 1)
                part_b1(t - 1, g)
                part_b2(t - 1, g)
            part_a2(NT - 1)
            part_b1(NT - 1, 2 + TG * (NT - 1) - 2)
            part_b2(NT - 1, 2 + TG * (NT - 1) - 2)

        @block.vector
        def _(dve):
            ch = Chain(dve, dve_step)

            def turn(dst, src, heads, half, table, tile):
                w = 4 * half
                cos = table[:, bass.ds(tile, 1), 0, :].to_broadcast([P, heads, w])
                sin = table[:, bass.ds(tile, 1), 1, :].to_broadcast([P, heads, w])
                a, b = r_a[:, 0:heads, 0:w], r_b[:, 0:heads, 0:w]
                ch.step(nc.vector.tensor_tensor(a, src, cos, ALU.mult))
                for part in range(2):
                    for h in range(2):
                        o, i = part * 2 * half + h * half, part * 2 * half + (1 - h) * half
                        last = ch.step(nc.vector.tensor_tensor(b[:, :, o:o + half], src[:, :, i:i + half],
                                                               sin[:, :, o:o + half], ALU.mult))
                dve.wait_ge(dve_step, last)
                ch.link(nc.vector.tensor_tensor(dst, a, b, ALU.add))

            def part_a1(t, g):
                dve.wait_ge(t_full, g + 2)
                dve.wait_ge(z_full, 3 * t)
                for k in range(4, KC):
                    ins = nc.vector.tensor_scalar(hT[:, k, :], tp[1][:, k - 4, :],
                                                  modt[:, bass.ds(t, 1), 1, k:k + 1].rearrange("p a b -> p (a b)"),
                                                  modt[:, bass.ds(t, 1), 0, k:k + 1].rearrange("p a b -> p (a b)"),
                                                  ALU.mult, ALU.add)
                ins.then_inc(freed[1], 1)

            def part_b1(t, g):
                dve.wait_ge(t_full, g + 4)
                dve.wait_ge(up_full, 4 * t)
                nc.vector.tensor_copy(qaT[:, 3:5, :], tp[1][:, 0:2, :]).then_inc(freed[1], 1)
                turn(g_tok[:, :, :], gn[:, :, :], G_ALL, HD // 4, rope_gqa, t)
                dve.wait_ge(up_act, 3 * t + 2)
                r = q_tok[:, :, NOPE:QK]
                turn(r, r, H_MLA + 1, ROPE // 4, rope_mla, t)
                dve.wait_ge(up_full, 4 * t + 4)
                kv = up[:, 0, :].rearrange("p (h d) -> p h d", h=4)
                nc.vector.tensor_copy(k_tok[:, 4:8, 0:NOPE], kv[:, :, 0:NOPE])
                dve.wait_ge(q_stored, 16 * NST * t)
                nc.vector.tensor_copy(v[:, 4 * VD:8 * VD].rearrange("p (h d) -> p h d", h=4),
                                      kv[:, :, NOPE:NOPE + VD]).then_inc(up_dve, 1)
                ch.step(nc.vector.tensor_copy(v[:, 8 * VD:10 * VD], vg[:, :]))
                dve.wait_ge(g_hi, t + 1)
                ch.step(nc.vector.tensor_tensor(gq2[:, :, 1, :], g_tok[:, 0:H_GQA, :], gq2[:, :, 0, :].bitcast(F32), ALU.subtract))
                ch.step(nc.vector.tensor_tensor(gk2[:, 1, :, :, :], g_tok[:, H_GQA:G_ALL, :].unsqueeze(2).to_broadcast([P, H_KV, 2, HD]),
                                                gk2[:, 0, :, :, :].bitcast(F32), ALU.subtract))
                ch.link(nc.vector.tensor_copy(k_tok[:, :, NOPE:QK],
                                              q_tok[:, H_MLA:H_MLA + 1, NOPE:QK].to_broadcast([P, H_MLA, ROPE])))

            def part_a2(t):
                for n in (1, 2):
                    dve.wait_ge(z_full, 3 * t + n + 1)
                    nc.vector.tensor_copy(z[:, n * ZW:(n + 1) * ZW], zp[:, n, 0:ZW]).then_inc(z_out, 1)
                dve.wait_ge(z_out, 2 * t + 2)
                zg = z[:, Z_G:Z_V].rearrange("p (h d) -> p h d", d=HD)
                ch.link(nc.vector.scalar_tensor_tensor(sq[:, :, :], zg, 1.0 / HD, zg, ALU.mult, ALU.mult))
                nc.vector.tensor_reduce(ms[:, 2:2 + G_ALL], sq[:, :, :], AX.X, ALU.add).then_inc(norm_in, 1)
                ch.step(nc.vector.tensor_copy(vg[:, :], z[:, Z_V:Z_ALL]))
                ch.step(nc.vector.tensor_copy(q_tok[:, H_MLA, NOPE:QK], z[:, Z_KR:Z_G]))
                dve.wait_ge(norm_out, t + 1)
                ch.link(nc.vector.tensor_tensor(gn[:, :, :], zg,
                                                rstd[:, 2:2 + G_ALL].unsqueeze(2).to_broadcast([P, G_ALL, HD]), ALU.mult))
                ch.link(nc.vector.tensor_tensor(gn[:, :, :], gn[:, :, :], g_row[:, :, :], ALU.mult))

            def part_b2(t, g):
                dve.wait_ge(q_stored, 16 * NST * t)
                for n, dst in enumerate((kT, kT, qT, qT)):
                    h0 = 4 * (n % 2)
                    dve.wait_ge(hi_done, 4 * t + n + 1)
                    nc.vector.tensor_tensor(dst[1][:, h0:h0 + 4, :], tp[n % 2][0:QK, :, :],
                                            dst[0][:, h0:h0 + 4, :].bitcast(F32), ALU.subtract).then_inc(freed[n % 2], 1)
                dve.wait_ge(t_full, g + 10)
                nc.vector.tensor_copy(gqT[:, 4:8, :], tp[1][:, :, :]).then_inc(freed[1], 1)
                dve.wait_ge(t_full, g + 12)
                nc.vector.tensor_copy(gkT[:, 2:4, :], tp[1][:, 0:2, :]).then_inc(freed[1], 1)

            dve.wait_ge(prep, 128)
            dve.wait_ge(modt_ready, 1)
            ch.step(nc.vector.tensor_scalar(modt[:, :, 1, :], modt[:, :, 1, :], 1.0, None, ALU.add))
            ch.step(nc.vector.tensor_scalar(g_row[:, 0:H_GQA, :], r_a[:, 0:1, :].to_broadcast([P, H_GQA, HD]),
                                            GQA_SCALE, None, ALU.mult))
            ch.step(nc.vector.tensor_copy(g_row[:, H_GQA:G_ALL, :], r_a[:, 1:2, :].to_broadcast([P, H_KV, HD])))
            dve.wait_ge(w_loaded, 48)
            dve.wait_ge(t_loaded, 32)
            for k in range(3):
                ch.step(nc.vector.tensor_scalar(w_q[:, k, :], w_q[:, k, :], g_col[:, k:k + 1], None, ALU.mult))
            for k in range(2):
                ch.step(nc.vector.tensor_scalar(w_kv[:, k, :], w_kv[:, k, :], g_col[:, 3 + k:4 + k], None, ALU.mult))
            assert ch.n == PRE
            part_a1(0, 0)
            with dve.Fori(1, NT) as t:
                g = 2 + TG * (t - 1)
                ch.start((t - 1) * (A2 + B1) + PRE)
                part_a1(t, g)
                part_a2(t - 1)
                assert ch.n == A2
                part_b1(t - 1, g)
                assert ch.n == A2 + B1
                part_b2(t - 1, g)
            ch.start(PRE + (NT - 1) * (A2 + B1))
            part_a2(NT - 1)
            part_b1(NT - 1, 2 + TG * (NT - 1) - 2)
            part_b2(NT - 1, 2 + TG * (NT - 1) - 2)

        @block.tensor
        def _(pe):
            ident = C["ident"]

            def bank_free(b, n):
                pe.wait_ge(freed[b], n)

            def part_x(t, taken):
                pe.wait_ge(x_loaded, 16 * (t + 1))
                for b in range(2):
                    bank_free(b, taken)
                    for k in range(4):
                        ins = nc.tensor.transpose(tp[b][:, k, :], xt[:, bass.ts(4 * b + k, P)], ident[:, :])
                    ins.then_inc(t_full, 1)

            def groups(jobs, taken, between=None):
                for n, job in enumerate(jobs):
                    b = n % 2
                    bank_free(b, taken + n // 2)
                    for k, (src, rows) in enumerate(job):
                        ins = nc.tensor.transpose(tp[b][0:rows, k, :], src, ident[:, :])
                    ins.then_inc(t_full, 1)
                    if between:
                        between(n)

            def part_z(t, n, taken=None, chunks=range(KC)):
                if taken is not None:
                    bank_free(0, taken + 1)
                    bank_free(1, taken + 1)
                if 0 in chunks:
                    if n == 0:
                        pe.wait_ge(z_act, t)
                    else:
                        pe.wait_ge(z_out, 2 * t)
                for k in chunks:
                    ins = nc.tensor.matmul(zp[:, n, 0:ZW], hT[:, k, :], w_in[:, k, n * ZW:(n + 1) * ZW],
                                           start=(k == 0), stop=(k == KC - 1))
                if KC - 1 in chunks:
                    ins.then_inc(z_full, 1)

            def part_b1(t, taken):
                pe.wait_ge(qa_ready, t + 1)
                groups([[(qa[:, k, :], P) for k in range(3)], [(qa[:, k, :], P) for k in (3, 4)]], taken)

            def part_up(t, taken):
                bank_free(0, taken + 1)
                HW = 4 * QK
                for n in range(2):
                    if n == 0:
                        pe.wait_ge(up_act, 3 * t)
                        pe.wait_ge(up_dve, t)
                    for k in range(3):
                        ins = nc.tensor.matmul(up[:, n, 0:HW], qaT[:, k, :], w_q[:, k, n * HW:(n + 1) * HW],
                                               start=(k == 0), stop=(k == 2))
                    ins.then_inc(up_full, 1)
                bank_free(1, taken + 1)
                for n, b in ((0, 2), (1, 0)):
                    if n == 1:
                        pe.wait_ge(up_act, 3 * t + 1)
                    for k in range(2):
                        ins = nc.tensor.matmul(up[:, b, :], qaT[:, 3 + k, :], w_kv[:, k, n * 512:(n + 1) * 512],
                                               start=(k == 0), stop=(k == 1))
                    ins.then_inc(up_full, 1)

            def part_heads(t, taken, between=None):
                pe.wait_ge(dve_step, PRE + A2 + B1 + t * (A2 + B1))
                pe.wait_ge(up_act, 3 * t + 3)
                pe.wait_ge(up_dve, t + 1)
                gg = gq2[:, :, :, :].bitcast(F32).rearrange("p h a d -> p (h a d)")
                kk = gk2[:, :, :, :, :].bitcast(F32).rearrange("p a h b d -> p (a h b d)")
                groups([[(k_tok[:, h, :], QK) for h in range(4)], [(k_tok[:, h, :], QK) for h in range(4, 8)],
                           [(q_tok[:, h, :], QK) for h in range(4)], [(q_tok[:, h, :], QK) for h in range(4, 8)],
                           [(gg[:, bass.ts(j, P)], P) for j in range(4)], [(gg[:, bass.ts(j, P)], P) for j in range(4, 8)],
                           [(kk[:, bass.ts(j, P)], P) for j in range(2)], [(kk[:, bass.ts(j, P)], P) for j in range(2, 4)]], taken, between)

            pe.wait_ge(dve_step, PRE)
            pe.wait_ge(w_loaded, 48)
            part_x(0, 0)
            for n in range(3):
                part_z(0, n, 0 if n == 0 else None)
            with pe.Fori(1, NT) as t:
                taken = 1 + 6 * (t - 1)
                part_x(t, taken)
                part_z(t, 0, taken)
                part_b1(t - 1, taken + 1)
                part_up(t - 1, taken + 1)
                part_z(t, 1)
                part_heads(t - 1, taken + 2, lambda k: part_z(t, 2, chunks=[k]))
            taken = 1 + 6 * (NT - 1)
            part_b1(NT - 1, taken)
            part_up(NT - 1, taken)
            part_heads(NT - 1, taken + 1)



def load_keys_values(nc, S, KV, sp):
    for j in range(H_MLA // 2):
        for n in range(2):
            sp.dma_start(KV["k_mla"][n][:, 2 * j:2 * j + 2, :].bitcast(F32),
                         S["k_mla"][n, :, 2 * j:2 * j + 2, :]).then_inc(KV["k_loaded"][j], 16)
        if j == 0:
            sp.dma_start(KV["v"][:, :, :], S["v_s"].rearrange("(t p) n -> p t n", p=P)).then_inc(KV["v_loaded"], 16)
    sp.dma_start(KV["k_gqa"][:, :, :].bitcast(F32), S["k_gqa"]).then_inc(KV["k_loaded"][H_MLA // 2], 16)


def attention(nc, S, C, KV, layer, tiles, kb, name):
    first, last_tile = tiles
    turns = (last_tile - first) // 2
    UNITS, STEPS = HEADS // 2, 2 * HEADS
    GRP = [(0, 4), (4, 7), (7, 10)] if kb == 10 else [(0, kb)]
    assert GRP[-1][1] == kb
    NG = len(GRP)
    PIECES = [(a, min(a + 512, kb * P)) for a in range(0, kb * P, 512)]
    SHARE = [range(kb * i // 4, kb * (i + 1) // 4) for i in range(4)]
    with ExitStack() as cx:
        new_semaphore = cx.enter_context(semaphores(nc))

        def sb(n, shape, dt=F32):
            return cx.enter_context(nc.sbuf_tensor(f"{n}_{name}{layer}", shape, dt))

        def sem(n):
            return new_semaphore(f"{n}_{name}{layer}")

        qm = [sb(f"qm{n}", [QK, 2, H_MLA, P], F32R) for n in range(2)]
        qg = sb("qg", [P, 2, H_GQA, P], F32R)
        pr = sb("pr", [P, 2, kb * P])
        pt = sb("pt", [P, 2, kb, 2, 2 * P])
        nmax = sb("nmax", [P, 2])
        rsum = sb("rsum", [P, 8])
        rinv = sb("rinv", [P, 4])
        diag = sb("diag", [P, 4, P])
        ot = sb("ot", [P, 2, P])
        sc = cx.enter_context(nc.psum_tensor(f"sc_{name}{layer}", [P, 2, 1536], F32))
        tp = cx.enter_context(nc.psum_tensor(f"tp_{name}{layer}", [P, 4, P], F32))
        op = cx.enter_context(nc.psum_tensor(f"op_{name}{layer}", [P, 2, 2 * P], F32))
        qm_loaded, qg_loaded, o_stored = sem("qm_loaded"), sem("qg_loaded"), sem("o_stored")
        s_full, max_done, exp_done = sem("s_full"), sem("max_done"), sem("exp_done")
        t_full, t_dve, t_act = sem("t_full"), sem("t_dve"), sem("t_act")
        inv_done, diag_done = sem("inv_done"), sem("diag_done")
        v_done, r_full, r_out, o_out = sem("v_done"), sem("r_full"), sem("r_out"), sem("o_out")
        rb = sb("rb", [P, 2 * P])
        block = cx.enter_context(nc.Block())
        N_DVE = min(NG, 2)

        def place(n):
            return n // 4, n % 4 // 2, n % 2

        @block.sync
        def _(sp):
            def q_rows(t, n):
                return S["q_mla"][bass.ds(2 * t + first, 2), n].rearrange("a p h n -> p a h n")

            def body(t):
                if not isinstance(t, int):
                    sp.wait_ge(s_full, STEPS * (t - 1) + 2 * H_MLA)
                for n in range(2):
                    for a in range(2):
                        sp.dma_start(qm[n][:, a].bitcast(F32), S["q_mla"][bass.ds(2 * t + (first + a), 1), n]
                                     .rearrange("a p h n -> p (a h) n")).then_inc(qm_loaded, 16)
                if not isinstance(t, int):
                    sp.wait_ge(s_full, STEPS * t)
                for a in range(2):
                    sp.dma_start(qg[:, a].bitcast(F32), S["q_gqa"][bass.ds(2 * t + (first + a), 1)]
                                 .rearrange("a p h n -> p (a h) n")).then_inc(qg_loaded, 16)
                if isinstance(t, int) and KV["fresh"]:
                    load_keys_values(nc, S, KV, sp)

            body(0)
            if turns > 1:
                with sp.Fori(1, turns) as t:
                    body(t)

        @block.tensor
        def _(pe):
            def scores(t, n, pieces):
                unit, hh, a = place(n)
                h = 2 * unit + hh
                if pieces[0] == 0:
                    if n % 4 == 0:
                        if h < H_MLA:
                            pe.wait_ge(KV["k_loaded"][unit], 32)
                        if h == 0:
                            pe.wait_ge(qm_loaded, 64 * (t + 1))
                        if h == H_MLA:
                            pe.wait_ge(KV["k_loaded"][H_MLA // 2], 16)
                            pe.wait_ge(qg_loaded, 32 * (t + 1))
                    pe.wait_ge(exp_done, STEPS * t + max(n - 1, 0))
                if h < H_MLA:
                    pairs = [(qm[x][:, a, h, :], KV["k_mla"][y][:, h, :]) for x, y in ((0, 0), (0, 1), (1, 0))]
                else:
                    g = h - H_MLA
                    pairs = [(qg[:, a, g, :], KV["k_gqa"][:, x * H_KV + g // (H_GQA // H_KV), :]) for x in range(2)]
                for p in pieces:
                    lo, hi = PIECES[p]
                    for m, (q, k) in enumerate(pairs):
                        ins = nc.tensor.matmul(sc[:, n % 2, lo:hi], q, k[:, lo:hi], start=(m == 0), stop=(m == len(pairs) - 1))
                if pieces[-1] == len(PIECES) - 1:
                    ins.then_inc(s_full, 1)

            def transposes(t, n, g):
                if g == 0:
                    pe.wait_ge(exp_done, STEPS * t + n + 1)
                    if NG == 3:
                        pe.wait_ge(t_act, STEPS * t + n)
                    else:
                        pe.wait_ge(t_dve, N_DVE * (STEPS * t + n))
                else:
                    pe.wait_ge(t_dve, N_DVE * (STEPS * t + n) + g)
                lo, hi = GRP[g]
                for k in range(lo, hi):
                    ins = nc.tensor.transpose(tp[:, k - lo, :], pr[:, n % 2, k * P:(k + 1) * P], C["ident"][:, :])
                ins.then_inc(t_full, 1)

            def values(t, unit, blocks):
                if 0 in blocks:
                    if unit == 0:
                        pe.wait_ge(KV["v_loaded"], 16)
                    pe.wait_ge(t_dve, N_DVE * (STEPS * t + 4 * unit + 4))
                    if NG == 3:
                        pe.wait_ge(t_act, STEPS * t + 4 * unit + 4)
                    pe.wait_ge(o_out, UNITS * t + unit)
                for k in blocks:
                    for hh in range(2):
                        h = 2 * unit + hh
                        col = h if h < H_MLA else H_MLA + (h - H_MLA) // (H_GQA // H_KV)
                        ins = nc.tensor.matmul(op[VD * hh:VD * hh + VD, 0, :], KV["v"][:, k, col * VD:(col + 1) * VD],
                                               pt[:, unit % 2, k, hh, :], start=(k == 0), stop=(k == kb - 1))
                if kb - 1 in blocks:
                    ins.then_inc(v_done, 1)

            def sums(t, unit):
                pe.wait_ge(diag_done, UNITS * t + unit + 1)
                for a in range(2):
                    for hh in range(2):
                        ins = nc.tensor.matmul(op[VD * hh:VD * hh + VD, 1, a * P:(a + 1) * P], C["ones"][:, 0:VD],
                                               diag[:, 2 * hh + a, :], start=True, stop=True)
                ins.then_inc(r_full, 1)

            with pe.Fori(0, turns) as t:
                every = list(range(len(PIECES)))
                scores(t, 0, every)
                scores(t, 1, every)
                for n in range(STEPS):
                    for i in range(3):
                        if i < NG:
                            transposes(t, n, i)
                        if n + 2 < STEPS and i < len(PIECES):
                            scores(t, n + 2, [i])
                    if n >= 4:
                        if SHARE[n % 4]:
                            values(t, n // 4 - 1, SHARE[n % 4])
                        if n % 4 == 3:
                            sums(t, n // 4 - 1)
                values(t, UNITS - 1, range(kb))
                sums(t, UNITS - 1)

        @block.scalar
        def _(act):
            def exponential(t, n):
                act.wait_ge(max_done, STEPS * t + n + 1)
                act.wait_ge(t_full, NG * (STEPS * t + max(n - 1, 0)))
                act.wait_ge(inv_done, STEPS * t + max(n - 7, 0))
                nc.scalar.activation(pr[:, n % 2, :], sc[:, n % 2, 0:kb * P], ACT.Exp, bias=nmax[:, n % 2:n % 2 + 1],
                                     accum_out=rsum[:, n % 8:n % 8 + 1]).then_inc(exp_done, 1)

            def spread(t, unit):
                act.wait_ge(r_full, UNITS * t + unit + 1)
                act.wait_ge(o_out, UNITS * t + unit)
                nc.scalar.activation(rb[:, :], op[:, 1, :], ACT.Copy).then_inc(r_out, 1)

            with act.Fori(0, turns) as t:
                exponential(t, 0)
                for n in range(STEPS):
                    if n + 1 < STEPS:
                        exponential(t, n + 1)
                    if n % 4 == 0 and n >= 8:
                        spread(t, n // 4 - 2)
                    if NG == 3:
                        unit, hh, a = place(n)
                        act.wait_ge(t_full, NG * (STEPS * t + n + 1))
                        act.wait_ge(v_done, UNITS * t + max(unit - 1, 0))
                        lo, hi = GRP[2]
                        nc.scalar.activation(pt[:, unit % 2, lo:hi, hh, a * P:(a + 1) * P], tp[:, 0:hi - lo, :],
                                             ACT.Copy).then_inc(t_act, 1)
                for unit in (UNITS - 2, UNITS - 1):
                    spread(t, unit)

        @block.vector
        def _(dve):
            def maximum(t, n):
                dve.wait_ge(s_full, STEPS * t + n + 1)
                dve.wait_ge(exp_done, STEPS * t + max(n - 1, 0))
                nc.vector.tensor_reduce(nmax[:, n % 2:n % 2 + 1], sc[:, n % 2, 0:kb * P], AX.X, ALU.max,
                                        negate=True).then_inc(max_done, 1)

            def take(t, n, g):
                unit, hh, a = place(n)
                dve.wait_ge(t_full, NG * (STEPS * t + n) + g + 1)
                dve.wait_ge(v_done, UNITS * t + max(unit - 1, 0))
                lo, hi = GRP[g]
                nc.vector.tensor_copy(pt[:, unit % 2, lo:hi, hh, a * P:(a + 1) * P], tp[:, 0:hi - lo, :]).then_inc(t_dve, 1)

            def diagonals(t, unit):
                dve.wait_ge(exp_done, STEPS * t + 4 * unit + 4)
                for i in range(4):
                    c = (4 * unit + i) % 8
                    nc.vector.reciprocal(rinv[:, i:i + 1], rsum[:, c:c + 1]).then_inc(inv_done, 1)
                dve.wait_ge(inv_done, STEPS * t + 4 * unit + 4)
                dve.wait_ge(r_full, UNITS * t + unit)
                for i in range(4):
                    ins = nc.vector.tensor_scalar(diag[:, i, :], C["ident"][:, :], rinv[:, i:i + 1], None, ALU.mult)
                ins.then_inc(diag_done, 1)

            def output(t, unit):
                dve.wait_ge(v_done, UNITS * t + unit + 1)
                dve.wait_ge(r_out, UNITS * t + unit + 1)
                dve.wait_ge(o_stored, 32 * (UNITS * t + unit))
                nc.vector.tensor_tensor(ot[:, :, :], op[:, 0, :].rearrange("p (a n) -> p a n", a=2),
                                        rb[:, :].rearrange("p (a n) -> p a n", a=2), ALU.mult).then_inc(o_out, 1)

            with dve.Fori(0, turns) as t:
                maximum(t, 0)
                for n in range(STEPS):
                    if n + 1 < STEPS:
                        maximum(t, n + 1)
                    take(t, n, 0)
                    if n % 4 == 0 and n >= 8:
                        output(t, n // 4 - 2)
                    if NG == 3:
                        take(t, n, 1)
                    if n % 4 == 2 and n >= 4:
                        diagonals(t, n // 4 - 1)
                output(t, UNITS - 2)
                diagonals(t, UNITS - 1)
                output(t, UNITS - 1)

        @block.gpsimd
        def _(pool):
            with pool.Fori(0, turns) as t:
                for unit in range(UNITS):
                    pool.wait_ge(o_out, UNITS * t + unit + 1)
                    for a in range(2):
                        pool.dma_start(S["o_s"][bass.ds(2 * t + (first + a), 1), :, unit, :].rearrange("a p n -> p (a n)"),
                                       ot[:, a, :]).then_inc(o_stored, 16)
            pool.wait_ge(o_stored, 32 * UNITS * turns)



def norm_steps(nc, dve, ch, u, stats, mv, rs_wait, gain, bias, out, filler):
    for n in range(2):
        ch.step(nc.vector.bn_stats(stats[:, n, :], u[:, n * 512:(n + 1) * 512]))
    dve.wait_ge(ch.sem, ch.base + ch.n)
    nc.vector.memset(filler, 0.0)
    rstd = rs_wait(nc.vector.bn_aggr(mv[:, :], stats[:, :, :]))
    ch.link(nc.vector.tensor_scalar(u[:, :], u[:, :], mv[:, 0:1], rstd, ALU.subtract, ALU.mult))
    ch.link(nc.vector.tensor_tensor(u[:, :], u[:, :], gain, ALU.mult))
    return nc.vector.tensor_tensor(out, u[:, :], bias, ALU.add)


def pool_rstd(nc, pool, C, mv, veps, rstd, mv_ready, eps_done, rstd_ready, t):
    pool.wait_ge(mv_ready, t + 1)
    nc.gpsimd.tensor_tensor(veps[:, :], mv[:, 1:2], C["eps"][:, 15:16], ALU.add).then_inc(eps_done, 1)
    pool.wait_ge(eps_done, t + 1)
    nc.gpsimd.tensor_tensor(rstd[:, :], veps[:, :], C["mhalf"][:, 0:1], ALU.pow).then_inc(rstd_ready, 1)



def mix_and_route(nc, A, S, C, LG, layer, stream):
    first, end = (0, CT) if stream == 0 else (CT, NT)
    n_tiles = end - first
    NR = NGRP + NE
    name = f"{'ctx' if stream == 0 else 'lat'}{layer}"
    with ExitStack() as cx:
        new_semaphore = cx.enter_context(semaphores(nc))

        def sb(n, shape):
            return cx.enter_context(nc.sbuf_tensor(f"mr_{n}_{name}", shape, F32))

        def sem(n):
            return new_semaphore(f"mr_{n}_{name}")

        w_o = sb("w_o", [P, KC, D])
        w_r = sb("w_r", [P, KC, NR])
        b_r = sb("b_r", [P, NR])
        bc = sb("bc", [P, 5, D])
        ot = sb("ot", [P, KC, P])
        xt = sb("xt", [P, D])
        oT = sb("oT", [P, KC, P])
        u = sb("u", [P, D])
        x1 = sb("x1", [P, D])
        h = sb("h", [P, D])
        hT = sb("hT", [P, KC, P])
        stats = sb("stats", [P, 2, 6])
        mv = sb("mv", [P, 2])
        veps = sb("veps", [P, 1])
        rstd = sb("rstd", [P, 1])
        filler = sb("filler", [P, 1])
        tp = [cx.enter_context(nc.psum_tensor(f"mr_tp{b}_{name}", [P, 4, P], F32)) for b in range(2)]
        mp = cx.enter_context(nc.psum_tensor(f"mr_mp_{name}", [P, D], F32))
        rp = cx.enter_context(nc.psum_tensor(f"mr_rp_{name}", [P, 512], F32))
        w_loaded, v_loaded, o_loaded, x_loaded = sem("w_loaded"), sem("v_loaded"), sem("o_loaded"), sem("x_loaded")
        t_full, t_act, t_dve = sem("t_full"), sem("t_act"), sem("t_dve")
        o_taken = sem("o_taken")
        mix_full, r_full, steps = sem("mix_full"), sem("r_full"), sem("steps")
        mv_ready, eps_done, rstd_ready = sem("mv_ready"), sem("eps_done"), sem("rstd_ready")
        x1_ready, h_ready, out_stored = sem("x1_ready"), sem("h_ready"), sem("out_stored")
        block = cx.enter_context(nc.Block())
        STEPS = 9

        def row(ap, t):
            return ap.rearrange("(t p) n -> t p n", p=P)[bass.ds(t + first, 1)].rearrange("a p n -> p (a n)")

        @block.sync
        def _(sp):
            def load(t):
                sp.dma_start(ot[:, :, :], S["o_s"][bass.ds(t + first, 1)].rearrange("a p c n -> p (a c) n")).then_inc(o_loaded, 16)
            load(0)
            sp.dma_start(w_o[:, :, :], A["w_o"][layer].rearrange("(a p) n -> p a n", p=P)).then_inc(w_loaded, 16)
            with sp.Fori(1, n_tiles) as t:
                sp.wait_ge(o_taken, t)
                load(t)

        @block.gpsimd
        def _(pool):
            for n, part in enumerate((2, 3, 4)):
                c0 = layer * 6 * D + part * D
                pool.dma_start(bc[:, n, :], S["ada"][stream, c0:c0 + D].partition_broadcast(P)).then_inc(v_loaded, 16)
            pool.dma_start(bc[:, 3, :], A["ln1_g"][layer].partition_broadcast(P)).then_inc(v_loaded, 16)
            pool.dma_start(bc[:, 4, :], A["ln1_b"][layer].partition_broadcast(P)).then_inc(v_loaded, 16)
            pool.dma_start(w_r[:, :, 0:NGRP], A["w_router_grp"][layer].rearrange("(a p) n -> p a n", p=P)).then_inc(v_loaded, 16)
            pool.dma_start(w_r[:, :, NGRP:NR], A["w_router_exp"][layer].rearrange("(a p) n -> p a n", p=P)).then_inc(v_loaded, 16)
            pool.dma_start(b_r[:, 0:NGRP], A["b_router_grp"][layer].partition_broadcast(P)).then_inc(v_loaded, 16)
            pool.dma_start(b_r[:, NGRP:NR], A["b_router_exp"][layer].partition_broadcast(P)).then_inc(v_loaded, 16)
            with pool.Fori(0, n_tiles) as t:
                pool_rstd(nc, pool, C, mv, veps, rstd, mv_ready, eps_done, rstd_ready, t)

        @block.scalar
        def _(act):
            def take_o(t):
                act.wait_ge(o_loaded, 16 * (t + 1))
                act.wait_ge(mix_full, 2 * t)
                nc.scalar.activation(oT[:, :, :], ot[:, :, :], ACT.Copy).then_inc(o_taken, 1)

            def take_h(t):
                act.wait_ge(t_full, 2 * t + 1)
                nc.scalar.activation(hT[:, 0:4, :], tp[0][:, :, :], ACT.Copy).then_inc(t_act, 1)

            def load_x(t):
                act.dma_start(xt[:, :], row(S["x_s"], t)).then_inc(x_loaded, 16)

            def store(t):
                act.wait_ge(x1_ready, t + 1)
                act.dma_start(row(S["x_s"], t), x1[:, :]).then_inc(out_stored, 16)
                act.wait_ge(h_ready, t + 1)
                act.dma_start(row(S["h_s"], t), h[:, :]).then_inc(out_stored, 16)

            load_x(0)
            take_o(0)
            with act.Fori(1, n_tiles) as t:
                take_o(t)
                act.wait_ge(x1_ready, t)
                load_x(t)
                store(t - 1)
                take_h(t - 1)
            store(n_tiles - 1)
            take_h(n_tiles - 1)
            act.wait_ge(out_stored, 32 * n_tiles)

        @block.tensor
        def _(pe):
            def groups(src, t_taken):
                for b in range(2):
                    pe.wait_ge(t_act if b == 0 else t_dve, t_taken)
                    for k in range(4):
                        ins = nc.tensor.transpose(tp[b][:, k, :], src[:, bass.ts(4 * b + k, P)], C["ident"][:, :])
                    ins.then_inc(t_full, 1)

            def mix(t):
                pe.wait_ge(o_taken, t + 1)
                if not (isinstance(t, int) and t == 0):
                    pe.wait_ge(steps, STEPS * (t - 1) + 3)
                for n in range(2):
                    for k in range(KC):
                        ins = nc.tensor.matmul(mp[:, n * 512:(n + 1) * 512], oT[:, k, :], w_o[:, k, n * 512:(n + 1) * 512],
                                               start=(k == 0), stop=(k == KC - 1))
                    ins.then_inc(mix_full, 1)

            def route(t, taken):
                pe.wait_ge(h_ready, t + 1)
                groups(h, taken)
                pe.wait_ge(t_act, taken + 1)
                pe.wait_ge(t_dve, taken + 1)
                for k in range(KC):
                    ins = nc.tensor.matmul(rp[:, 0:NR], hT[:, k, :], w_r[:, k, :], start=(k == 0), stop=(k == KC - 1))
                ins.then_inc(r_full, 1)

            pe.wait_ge(w_loaded, 16)
            pe.wait_ge(v_loaded, 144)
            pe.wait_ge(steps, 1)
            mix(0)
            with pe.Fori(1, n_tiles) as t:
                mix(t)
                route(t - 1, t - 1)
            route(n_tiles - 1, n_tiles - 1)

        @block.vector
        def _(dve):
            ch = Chain(dve, steps)

            def take_h(t):
                dve.wait_ge(t_full, 2 * t + 2)
                nc.vector.tensor_copy(hT[:, 4:8, :], tp[1][:, :, :]).then_inc(t_dve, 1)

            def norm(t):
                ch.start(1 + STEPS * t)
                for n in range(2):
                    dve.wait_ge(mix_full, 2 * t + n + 1)
                    ch.step(nc.vector.tensor_tensor(u[:, n * 512:(n + 1) * 512], mp[:, n * 512:(n + 1) * 512],
                                                    bc[:, 0, n * 512:(n + 1) * 512], ALU.mult))
                dve.wait_ge(steps, ch.base + ch.n)
                dve.wait_ge(x_loaded, 16 * (t + 1))
                ch.link(nc.vector.scalar_tensor_tensor(u[:, :], xt[:, :], ALPHA, u[:, :], ALU.mult, ALU.add))

                def rs(ins):
                    ins.then_inc(mv_ready, 1)
                    dve.wait_ge(mv_ready, t + 1)
                    dve.wait_ge(rstd_ready, t + 1)
                    dve.wait_ge(out_stored, 32 * t)
                    return rstd[:, 0:1]

                norm_steps(nc, dve, ch, u, stats, mv, rs, bc[:, 3, :], bc[:, 4, :], x1[:, :], filler[:, :]).then_inc(x1_ready, 1)
                dve.wait_ge(x1_ready, t + 1)
                ch.link(nc.vector.tensor_tensor(h[:, :], x1[:, :], bc[:, 2, :], ALU.mult))
                assert ch.n == STEPS - 1
                nc.vector.tensor_tensor(h[:, :], h[:, :], bc[:, 1, :], ALU.add).then_inc(h_ready, 1)

            def logits(t):
                dve.wait_ge(r_full, t + 1)
                ch.step(nc.vector.tensor_tensor(LG[:, bass.ds(t + first, 1), :].rearrange("p a n -> p (a n)"), rp[:, 0:NR],
                                                b_r[:, :], ALU.add))

            dve.wait_ge(v_loaded, 144)
            ch.link(nc.vector.tensor_scalar(bc[:, 2, :], bc[:, 2, :], 1.0, None, ALU.add))
            norm(0)
            with dve.Fori(1, n_tiles) as t:
                take_h(t - 1)
                ch.start(STEPS * t)
                logits(t - 1)
                norm(t)
            take_h(n_tiles - 1)
            ch.start(STEPS * n_tiles)
            logits(n_tiles - 1)



def routing(nc, S, C, R, layer):
    t0 = 0 if layer < DEPTH - 1 else CT
    nt = NT - t0
    nb = n_blocks(nt)
    MAXB = nt
    with ExitStack() as cx:
        new_semaphore = cx.enter_context(semaphores(nc))

        def sb(n, shape, dt=F32):
            return cx.enter_context(nc.sbuf_tensor(f"rt_{n}{layer}", shape, dt))

        def sem(n):
            return new_semaphore(f"rt_{n}{layer}")

        T = {k: sb(f"t_{k}", list(C["dram"][k].shape)) for k in ("rev", "edges", "block_no", "upto")}
        h = sb("h", [P, nt, D])
        m = sb("m", [P, nt])
        m1 = sb("m1", [P, nt])
        m2 = sb("m2", [P, nt])
        q = sb("q", [P, nt])
        pstar = sb("pstar", [P, nt])
        e2 = sb("e2", [P, nt])
        r = sb("r", [P, nt, PER])
        ex = sb("ex", [P, nt, NGRP])
        ohg = sb("ohg", [P, nt, NGRP])
        oh = [sb(f"oh{k}", [P, nt, PER]) for k in range(TOPK)]
        sel = sb("sel", [P, nt, NGRP, PER])
        leg = sb("leg", [P, nt, PER])
        E = [sb(f"E{k}", [P, nt, NGRP, PER]) for k in range(TOPK)]
        cnt = sb("cnt", [P, nt, NE])
        big = sb("big", [P, NE * max(NE, nb + 1)])
        nbk = sb("nbk", [P, NE])
        endb = sb("endb", [P, NE])
        start = sb("start", [P, NE])
        total = sb("total", [P, NE])
        pos = sb("pos", [P, nt, NE])
        dest = sb("dest", [P, nt])
        blkf = sb("blkf", [P, nb + 2])
        pp = cx.enter_context(nc.psum_tensor(f"rt_pp{layer}", [P, 512], F32))
        tt = cx.enter_context(nc.psum_tensor(f"rt_tt{layer}", [P, 512], F32))
        h_loaded, step, shifted, exps = sem("h_loaded"), sem("step"), sem("shifted"), sem("exps")
        cnt_ready, prefix_done = sem("cnt_ready"), sem("prefix_done")
        idx_ready, scattered, tables = sem("idx_ready"), sem("scattered"), sem("tables")
        block = cx.enter_context(nc.Block())
        LG = R["lg"][:, t0:NT, :]

        @block.sync
        def _(sp):
            for k, tile in T.items():
                sp.dma_start(tile[(slice(None),) * len(tile.shape)], C["dram"][k]).then_inc(tables, 16)
            sp.dma_start(h[:, :, :], S["h_s"][t0 * P:NT * P, :].rearrange("(t p) n -> p t n", p=P)).then_inc(h_loaded, 16)

        @block.scalar
        def _(act):
            act.wait_ge(shifted, 1)
            nc.scalar.activation(ex[:, :, :], ex[:, :, :], ACT.Exp).then_inc(exps, 1)
            act.wait_ge(shifted, 2)
            nc.scalar.activation(e2[:, :], e2[:, :], ACT.Exp).then_inc(exps, 1)

        @block.tensor
        def _(pe):
            pe.wait_ge(cnt_ready, 1)
            for j in range(nt):
                for i in range(j):
                    nc.tensor.matmul(pp[:, j * NE:(j + 1) * NE], C["ones"][:, :], cnt[:, i, :], start=(i == 0), stop=False)
                nc.tensor.matmul(pp[:, j * NE:(j + 1) * NE], C["tri"][:, :], cnt[:, j, :], start=(j == 0), stop=True)
            for i in range(nt):
                ins = nc.tensor.matmul(tt[:, 0:NE], C["ones"][:, :], cnt[:, i, :], start=(i == 0), stop=(i == nt - 1))
            ins.then_inc(prefix_done, 1)

        @block.vector
        def _(dve):
            ch = Chain(dve, step)
            V = nc.vector

            def wide(ap, n):
                return ap.unsqueeze(2).to_broadcast([P, nt, n])

            def first_equal(out, x, mx, rev, n):
                rr = r[:, :, 0:n]
                ch.link(V.tensor_tensor(rr, x, wide(mx, n), ALU.is_equal))
                ch.link(V.tensor_tensor(rr, rr, rev.unsqueeze(1).to_broadcast([P, nt, n]), ALU.mult))
                ch.link(V.tensor_reduce(q[:, :], rr, AX.X, ALU.max))
                ch.link(V.tensor_tensor(out, rr, wide(q[:, :], n), ALU.is_equal))

            lg = LG[:, :, 0:NGRP]
            le = LG[:, :, NGRP:NGRP + NE].rearrange("p t (g x) -> p t g x", g=NGRP)
            dve.wait_ge(tables, 64)
            ch.link(V.tensor_reduce(m[:, :], lg, AX.X, ALU.max))
            V.tensor_tensor(ex[:, :, :], lg, wide(m[:, :], NGRP), ALU.subtract).then_inc(shifted, 1)
            first_equal(ohg[:, :, :], lg, m[:, :], T["rev"][:, PER - NGRP:PER], NGRP)
            ch.link(V.tensor_tensor(sel[:, :, :, :], le, ohg[:, :, :].unsqueeze(3).to_broadcast([P, nt, NGRP, PER]), ALU.mult))
            ch.link(V.tensor_reduce(leg[:, :, :], sel[:, :, :, :].rearrange("p t g x -> p t x g"), AX.X, ALU.add))
            ch.link(V.tensor_reduce(m1[:, :], leg[:, :, :], AX.X, ALU.max))
            first_equal(oh[0][:, :, :], leg[:, :, :], m1[:, :], T["rev"][:, :], PER)
            ch.link(V.scalar_tensor_tensor(leg[:, :, :], oh[0][:, :, :], -BIG, leg[:, :, :], ALU.mult, ALU.add))
            ch.link(V.tensor_reduce(m2[:, :], leg[:, :, :], AX.X, ALU.max))
            V.tensor_tensor(e2[:, :], m2[:, :], m1[:, :], ALU.subtract).then_inc(shifted, 1)
            first_equal(oh[1][:, :, :], leg[:, :, :], m2[:, :], T["rev"][:, :], PER)
            for k in range(TOPK):
                ch.link(V.tensor_tensor(E[k][:, :, :, :], ohg[:, :, :].unsqueeze(3).to_broadcast([P, nt, NGRP, PER]),
                                        oh[k][:, :, :].unsqueeze(2).to_broadcast([P, nt, NGRP, PER]), ALU.mult))
            e_of = [e[:, :, :, :].rearrange("p t g x -> p t (g x)") for e in E]
            V.tensor_tensor(cnt[:, :, :], e_of[0], e_of[1], ALU.add).then_inc(cnt_ready, 1)
            dve.wait_ge(exps, 1)
            ch.link(V.tensor_reduce(q[:, :], ex[:, :, :], AX.X, ALU.add))
            ch.link(V.reciprocal(pstar[:, :], q[:, :]))
            dve.wait_ge(exps, 2)
            ch.link(V.tensor_scalar(q[:, :], e2[:, :], 1.0, None, ALU.add))
            ch.link(V.reciprocal(m[:, :], q[:, :]))
            ch.link(V.tensor_tensor(R["wt"][:, 0, 0:nt], m[:, :], pstar[:, :], ALU.mult))
            ch.link(V.tensor_tensor(R["wt"][:, 1, 0:nt], R["wt"][:, 0, 0:nt], e2[:, :], ALU.mult))
            dve.wait_ge(prefix_done, 1)
            ch.link(V.tensor_copy(total[:, :], tt[:, 0:NE]))
            b3 = big[:, 0:NE * MAXB].rearrange("p (e j) -> p e j", e=NE)
            ch.link(V.tensor_tensor(b3, total[:, :].unsqueeze(2).to_broadcast([P, NE, MAXB]),
                                    T["edges"][:, 0:MAXB].unsqueeze(1).to_broadcast([P, NE, MAXB]), ALU.is_gt))
            ch.link(V.tensor_reduce(nbk[:, :], b3, AX.X, ALU.add))
            b3 = big[:, 0:NE * NE].rearrange("p (e j) -> p e j", e=NE)
            ch.link(V.tensor_tensor(b3, nbk[:, :].unsqueeze(1).to_broadcast([P, NE, NE]), T["upto"][:, :, :], ALU.mult))
            ch.link(V.tensor_reduce(endb[:, :], b3, AX.X, ALU.add))
            ch.link(V.tensor_tensor(start[:, :], endb[:, :], nbk[:, :], ALU.subtract))
            ch.link(V.tensor_scalar(start[:, :], start[:, :], float(P), None, ALU.mult))
            ch.link(V.tensor_tensor(pos[:, :, :], pp[:, 0:nt * NE].rearrange("p (t e) -> p t e", e=NE),
                                    start[:, :].unsqueeze(1).to_broadcast([P, nt, NE]), ALU.add))
            for k in range(TOPK):
                ch.link(V.tensor_tensor(cnt[:, :, :], pos[:, :, :], e_of[k], ALU.mult))
                ch.link(V.tensor_reduce(dest[:, :], cnt[:, :, :], AX.X, ALU.add))
                V.tensor_copy(R["idx"][:, k, 0:nt], dest[:, :]).then_inc(idx_ready, 1)
            b3 = big[:, 0:NE * (nb + 1)].rearrange("p (b e) -> p b e", e=NE)
            ch.link(V.tensor_tensor(b3, endb[:, :].unsqueeze(1).to_broadcast([P, nb + 1, NE]),
                                    T["block_no"][:, 0:nb + 1].unsqueeze(2).to_broadcast([P, nb + 1, NE]), ALU.is_le))
            ch.link(V.tensor_reduce(blkf[:, 0:nb + 1], b3, AX.X, ALU.add))
            ch.link(V.tensor_scalar(blkf[:, 0:nb + 1], blkf[:, 0:nb + 1], float(NE - 1), None, ALU.min))
            ch.link(V.tensor_copy(R["blk"][:, 1:nb + 2], blkf[:, 0:nb + 1]))
            ch.link(V.tensor_copy(R["blk"][:, 0:1], endb[:, NE - 1:NE]))

        @block.gpsimd
        def _(pool):
            pool.wait_ge(h_loaded, 16)
            for k in range(TOPK):
                pool.wait_ge(idx_ready, k + 1)
                for t in range(nt):
                    pool.indirect_dma_start(S["xb"][:, :], bass.IndirectOffsetOnAxis(R["idx"][:, k, t:t + 1], 0),
                                            h[:, t, :], None, bounds_check=S["xb"].shape[0] - 1).then_inc(scattered, 16)
            pool.wait_ge(scattered, 16 * TOPK * nt)



def experts(nc, A, S, C, R, layer):
    nb = n_blocks(NT if layer < DEPTH - 1 else LT)
    turns = (nb + 1) // 2
    FC = FF // P
    with ExitStack() as cx:
        new_semaphore = cx.enter_context(semaphores(nc))

        def sb(n, shape):
            return cx.enter_context(nc.sbuf_tensor(f"ex_{n}{layer}", shape, F32))

        def sem(n):
            return new_semaphore(f"ex_{n}{layer}")

        wg = sb("wg", [P, 2, KC, FF])
        wu = sb("wu", [P, 2, KC, FF])
        wd = sb("wd", [P, 2, FC, D])
        xb = sb("xb", [P, 2, D])
        xT = sb("xT", [P, KC, P])
        sg = sb("sg", [P, FF])
        hm = sb("hm", [P, FF])
        hT = sb("hT", [P, FC, P])
        y = sb("y", [P, D])
        tx = [cx.enter_context(nc.psum_tensor(f"ex_tx{b}_{layer}", [P, 4, P], F32)) for b in range(2)]
        th = cx.enter_context(nc.psum_tensor(f"ex_th{layer}", [P, FC, P], F32))
        gp = cx.enter_context(nc.psum_tensor(f"ex_gp{layer}", [P, FF], F32))
        vp = cx.enter_context(nc.psum_tensor(f"ex_vp{layer}", [P, FF], F32))
        yp = cx.enter_context(nc.psum_tensor(f"ex_yp{layer}", [P, D], F32))
        g_loaded, u_loaded, d_loaded, x_loaded = ([sem(f"{n}_loaded{u}") for u in range(2)] for n in "gudx")
        x_turned, xT_act, xT_dve = sem("x_turned"), sem("xT_act"), sem("xT_dve")
        g_full, u_full, y_full = ([sem(f"{n}_full{u}") for u in range(2)] for n in "guy")
        silu_done, hm_ready, h_turned, hT_ready = sem("silu_done"), sem("hm_ready"), sem("h_turned"), sem("hT_ready")
        y_act, y_dve, y_stored = sem("y_act"), sem("y_dve"), sem("y_stored")
        block = cx.enter_context(nc.Block())

        def filled(eng):
            return eng.value_load(R["blk"][0:1, 0:1], min_val=1, max_val=nb)

        @block.sync
        def _(sp):
            n = filled(sp)
            with sp.Fori(0, turns) as i:
                for u in range(2):
                    b = 2 * i + u
                    with sp.If(b < n):
                        e = sp.value_load(R["blk"][0:1, bass.ds(b + 1, 1)], min_val=0, max_val=NE - 1)
                        w = [A[k][layer][bass.ds(e, 1)].rearrange("e (a p) n -> p (e a) n", p=P) for k in ("w_gate", "w_up", "w_down")]
                        sp.wait_ge(g_full[u], i)
                        sp.dma_start(wg[:, u], w[0]).then_inc(g_loaded[u], 16)
                        sp.wait_ge(u_full[u], i)
                        sp.dma_start(wu[:, u], w[1]).then_inc(u_loaded[u], 16)
                        sp.wait_ge(y_full[u], i)
                        sp.dma_start(wd[:, u], w[2]).then_inc(d_loaded[u], 16)

        @block.gpsimd
        def _(pool):
            n = filled(pool)
            rows = S["xb"].rearrange("(b p) n -> b p n", p=P)
            for u in range(2):
                pool.dma_start(xb[:, u, :], rows[u]).then_inc(x_loaded[u], 16)
            with pool.Fori(0, turns) as i:
                for u in range(2):
                    b = 2 * i + u
                    with pool.If(b < n):
                        pool.wait_ge(x_turned, 2 * b + 2)
                        pool.dma_start(xb[:, u, :], rows[bass.ds(b + 2, 1)].rearrange("a p n -> p (a n)")).then_inc(x_loaded[u], 16)
                        pool.wait_ge(y_act, b + 1)
                        pool.wait_ge(y_dve, b + 1)
                        pool.dma_start(rows[bass.ds(b, 1)].rearrange("a p n -> p (a n)"), y[:, :]).then_inc(y_stored, 16)
            pool.wait_ge(y_stored, n * 16)

        @block.tensor
        def _(pe):
            def turn_x(u, loads, b):
                pe.wait_ge(x_loaded[u], 16 * loads)
                for k in range(2):
                    pe.wait_ge(xT_act if k == 0 else xT_dve, b)
                    for c in range(4):
                        ins = nc.tensor.transpose(tx[k][:, c, :], xb[:, u, bass.ts(4 * k + c, P)], C["ident"][:, :])
                    ins.then_inc(x_turned, 1)

            n = filled(pe)
            turn_x(0, 1, 0)
            with pe.Fori(0, turns) as i:
                for u in range(2):
                    b = 2 * i + u
                    with pe.If(b < n):
                        pe.wait_ge(xT_act, b + 1)
                        pe.wait_ge(xT_dve, b + 1)
                        pe.wait_ge(g_loaded[u], 16 * (i + 1))
                        pe.wait_ge(silu_done, b)
                        for k in range(KC):
                            ins = nc.tensor.matmul(gp[:, :], xT[:, k, :], wg[:, u, k, :], start=(k == 0), stop=(k == KC - 1))
                        ins.then_inc(g_full[u], 1)
                        pe.wait_ge(u_loaded[u], 16 * (i + 1))
                        pe.wait_ge(hm_ready, b)
                        for k in range(KC):
                            ins = nc.tensor.matmul(vp[:, :], xT[:, k, :], wu[:, u, k, :], start=(k == 0), stop=(k == KC - 1))
                        ins.then_inc(u_full[u], 1)
                        turn_x(1 - u, i + 1 + u, b + 1)
                        pe.wait_ge(hm_ready, b + 1)
                        pe.wait_ge(hT_ready, b)
                        for c in range(FC):
                            ins = nc.tensor.transpose(th[:, c, :], hm[:, bass.ts(c, P)], C["ident"][:, :])
                        ins.then_inc(h_turned, 1)
                        pe.wait_ge(hT_ready, b + 1)
                        pe.wait_ge(d_loaded[u], 16 * (i + 1))
                        pe.wait_ge(y_act, b)
                        pe.wait_ge(y_dve, b)
                        for m in range(2):
                            for c in range(FC):
                                ins = nc.tensor.matmul(yp[:, m * 512:(m + 1) * 512], hT[:, c, :], wd[:, u, c, m * 512:(m + 1) * 512],
                                                       start=(c == 0), stop=(c == FC - 1))
                        ins.then_inc(y_full[u], 1)

        @block.scalar
        def _(act):
            def take_x(b):
                act.wait_ge(x_turned, 2 * b + 1)
                nc.scalar.activation(xT[:, 0:4, :], tx[0][:, :, :], ACT.Copy).then_inc(xT_act, 1)

            n = filled(act)
            take_x(0)
            with act.Fori(0, turns) as i:
                for u in range(2):
                    b = 2 * i + u
                    with act.If(b < n):
                        act.wait_ge(g_full[u], i + 1)
                        act.wait_ge(hm_ready, b)
                        nc.scalar.activation(sg[:, :], gp[:, :], ACT.Silu).then_inc(silu_done, 1)
                        take_x(b + 1)
                        act.wait_ge(y_full[u], i + 1)
                        act.wait_ge(y_stored, 16 * b)
                        nc.scalar.activation(y[:, 0:512], yp[:, 0:512], ACT.Copy).then_inc(y_act, 1)

        @block.vector
        def _(dve):
            def take_x(b):
                dve.wait_ge(x_turned, 2 * b + 2)
                nc.vector.tensor_copy(xT[:, 4:8, :], tx[1][:, :, :]).then_inc(xT_dve, 1)

            n = filled(dve)
            take_x(0)
            with dve.Fori(0, turns) as i:
                for u in range(2):
                    b = 2 * i + u
                    with dve.If(b < n):
                        dve.wait_ge(u_full[u], i + 1)
                        dve.wait_ge(silu_done, b + 1)
                        dve.wait_ge(h_turned, b)
                        nc.vector.tensor_tensor(hm[:, :], sg[:, :], vp[:, :], ALU.mult).then_inc(hm_ready, 1)
                        take_x(b + 1)
                        dve.wait_ge(h_turned, b + 1)
                        nc.vector.tensor_copy(hT[:, :, :], th[:, :, :]).then_inc(hT_ready, 1)
                        dve.wait_ge(y_full[u], i + 1)
                        dve.wait_ge(y_stored, 16 * b)
                        nc.vector.tensor_copy(y[:, 512:D], yp[:, 512:D]).then_inc(y_dve, 1)



def combine(nc, A, S, C, R, layer, out):
    last = layer == DEPTH - 1
    t0 = CT if last else 0
    nt = NT - t0
    with ExitStack() as cx:
        new_semaphore = cx.enter_context(semaphores(nc))

        def sb(n, shape):
            return cx.enter_context(nc.sbuf_tensor(f"cb_{n}{layer}", shape, F32))

        def sem(n):
            return new_semaphore(f"cb_{n}{layer}")

        y = [sb(f"y{k}", [P, nt, D]) for k in range(TOPK)]
        bc = sb("bc", [P, 4, D])
        xt = sb("xt", [P, D])
        u = sb("u", [P, D])
        x2 = sb("x2", [P, D])
        stats = sb("stats", [P, 2, 6])
        mv = sb("mv", [P, 2])
        veps = sb("veps", [P, 1])
        rstd = sb("rstd", [P, 1])
        filler = sb("filler", [P, 1])
        gathered, w_loaded, x_loaded = [sem(f"gathered{t}") for t in range(nt)], sem("w_loaded"), sem("x_loaded")
        steps, mv_ready, eps_done, rstd_ready = sem("steps"), sem("mv_ready"), sem("eps_done"), sem("rstd_ready")
        x_used, x2_ready, out_stored = sem("x_used"), sem("x2_ready"), sem("out_stored")
        block = cx.enter_context(nc.Block())
        STEPS = 7

        @block.gpsimd
        def _(pool):
            for t in range(nt):
                for k in range(TOPK):
                    pool.indirect_dma_start(y[k][:, t, :], None, S["xb"][:, :],
                                            bass.IndirectOffsetOnAxis(R["idx"][:, k, t:t + 1], 0),
                                            bounds_check=S["xb"].shape[0] - 1).then_inc(gathered[t], 16)
            for t in range(nt):
                pool_rstd(nc, pool, C, mv, veps, rstd, mv_ready, eps_done, rstd_ready, t)

        @block.sync
        def _(sp):
            c0 = layer * 6 * D + 5 * D
            sp.dma_start(bc[:, 0, :], S["ada"][0, c0:c0 + D].partition_broadcast(P)).then_inc(w_loaded, 16)
            sp.dma_start(bc[:, 1, :], S["ada"][1, c0:c0 + D].partition_broadcast(P)).then_inc(w_loaded, 16)
            sp.dma_start(bc[:, 2, :], A["ln2_g"][layer].partition_broadcast(P)).then_inc(w_loaded, 16)
            sp.dma_start(bc[:, 3, :], A["ln2_b"][layer].partition_broadcast(P)).then_inc(w_loaded, 16)
            xs = S["x_s"].rearrange("(t p) n -> t p n", p=P)
            dst = (out[0] if last else S["x_s"]).rearrange("(t p) n -> t p n", p=P)
            with sp.Fori(0, nt) as t:
                sp.wait_ge(x_used, t)
                sp.dma_start(xt[:, :], xs[bass.ds(t + t0, 1)].rearrange("a p n -> p (a n)")).then_inc(x_loaded, 16)
                sp.wait_ge(x2_ready, t + 1)
                sp.dma_start(dst[bass.ds(t, 1)].rearrange("a p n -> p (a n)"), x2[:, :]).then_inc(out_stored, 16)
            sp.wait_ge(out_stored, 16 * nt)

        @block.vector
        def _(dve):
            ch = Chain(dve, steps)
            dve.wait_ge(w_loaded, 64)
            for gate, first, n in ((0, 0, CT), (1, CT, LT)):
                if last and gate == 0:
                    continue
                done = 0 if last else first
                for i in range(n):
                    t = i + done
                    dve.wait_ge(gathered[t], 16 * TOPK)
                    ch.start((i + done) * STEPS)
                    dve.wait_ge(x2_ready, t)
                    w = [R["wt"][:, k, bass.ds(t, 1)] for k in range(TOPK)]
                    ya, yc = (y[k][:, bass.ds(t, 1), :].rearrange("p a n -> p (a n)") for k in range(TOPK))
                    ch.link(nc.vector.tensor_scalar(u[:, :], ya, w[0], None, ALU.mult))
                    ch.link(nc.vector.scalar_tensor_tensor(u[:, :], yc, w[1], u[:, :], ALU.mult, ALU.add))
                    ch.link(nc.vector.tensor_tensor(u[:, :], u[:, :], bc[:, gate, :], ALU.mult))
                    dve.wait_ge(x_loaded, 16 * (t + 1))
                    nc.vector.scalar_tensor_tensor(u[:, :], xt[:, :], ALPHA, u[:, :], ALU.mult, ALU.add).then_inc(x_used, 1)
                    dve.wait_ge(x_used, t + 1)

                    def rs(ins):
                        ins.then_inc(mv_ready, 1)
                        dve.wait_ge(mv_ready, t + 1)
                        dve.wait_ge(rstd_ready, t + 1)
                        dve.wait_ge(out_stored, 16 * t)
                        return rstd[:, 0:1]

                    norm_steps(nc, dve, ch, u, stats, mv, rs, bc[:, 2, :], bc[:, 3, :], x2[:, :], filler[:, :]).then_inc(x2_ready, 1)
                    assert ch.n == STEPS



CONSTS = ("ident", "tri", "ones", "mhalf", "eps")


def backbone(nc, A, consts, out, stop=None):
    S = {}

    def dram(name, shape):
        S[name] = nc.dram_tensor(name, shape, F32, kind="Internal").ap()

    dram("x_s", [NT * P, D])
    dram("h_s", [NT * P, D])
    dram("o_s", [NT, P, KC, P])
    dram("ada", [2, DEPTH * 6 * D])
    dram("q_mla", [NT, 2, QK, H_MLA, P])
    dram("q_gqa", [NT, P, H_GQA, P])
    dram("k_mla", [2, QK, H_MLA, NT * P])
    dram("k_gqa", [P, 2 * H_KV, NT * P])
    dram("v_s", [NT * P, (H_MLA + H_KV) * VD])
    dram("xb", [(NBP + 2) * P, D])
    with ExitStack() as cx:
        C = {k: cx.enter_context(nc.sbuf_tensor(f"c_{k}", list(consts[k].shape), F32)) for k in CONSTS}
        C["dram"] = consts
        C["xb_zeroed"] = cx.enter_context(nc.semaphore("xb_zeroed"))
        R = {"lg": cx.enter_context(nc.sbuf_tensor("logits", [P, NT, NGRP + NE], F32)),
             "wt": cx.enter_context(nc.sbuf_tensor("weights", [P, TOPK, NT], F32)),
             "idx": cx.enter_context(nc.sbuf_tensor("slots", [P, TOPK, NT], I32)),
             "blk": cx.enter_context(nc.sbuf_tensor("blocks", [P, NB + 3], I32))}
        loaded = cx.enter_context(nc.semaphore("consts_loaded"))
        with nc.Block() as block:
            @block.sync
            def _(sp):
                for k in CONSTS:
                    n = len(consts[k].shape)
                    at = (slice(None),) * n
                    sp.dma_start(C[k][at], consts[k]).then_inc(loaded, 16)
                sp.wait_ge(loaded, 16 * len(CONSTS))
        modulation(nc, A, S)
        if stop == "ada":
            return S
        for layer in range(DEPTH):
            with nc.sbuf_tensor(f"zeros{layer}", [P, D if layer == 0 else 8], F32) as zeros:
                C["zeros"] = zeros
                projections(nc, A, S, C, layer)
            if stop == "proj":
                return S
            with ExitStack() as kx:
                new_semaphore = kx.enter_context(semaphores(nc))
                KV = {"k_mla": [kx.enter_context(nc.sbuf_tensor(f"k_mla{n}_{layer}", [QK, H_MLA, NT * P], F32R)) for n in range(2)],
                      "k_gqa": kx.enter_context(nc.sbuf_tensor(f"k_gqa{layer}", [P, 2 * H_KV, NT * P], F32R)),
                      "v": kx.enter_context(nc.sbuf_tensor(f"v_all{layer}", [P, NT, (H_MLA + H_KV) * VD], F32)),
                      "k_loaded": [new_semaphore(f"k_loaded{j}_{layer}") for j in range(H_MLA // 2 + 1)],
                      "v_loaded": new_semaphore(f"v_loaded{layer}"), "fresh": True}
                if layer < DEPTH - 1:
                    attention(nc, S, C, KV, layer, (0, CT), CT, "ctx")
                    KV["fresh"] = False
                attention(nc, S, C, KV, layer, (CT, NT), NT, "lat")
            if stop == "attn":
                return S
            if layer < DEPTH - 1:
                mix_and_route(nc, A, S, C, R["lg"], layer, 0)
            mix_and_route(nc, A, S, C, R["lg"], layer, 1)
            if stop == "mix":
                return S
            routing(nc, S, C, R, layer)
            if stop == "route":
                return S
            experts(nc, A, S, C, R, layer)
            combine(nc, A, S, C, R, layer, out)
            if stop == "layer0":
                return S
    return S


_INS = ["x", "c", "ctx", "c_ctx", "w_ada", "b_ada", "w_in", "g_q_a", "w_q_b", "g_kv_a", "w_kv_b", "g_gqa_q", "g_gqa_k",
        "w_o", "ln1_g", "ln1_b", "w_router_grp", "b_router_grp", "w_router_exp", "b_router_exp",
        "w_gate", "w_up", "w_down", "ln2_g", "ln2_b"]


def constants():
    f = np.float32
    i = np.arange(P)
    c = {"ident": np.eye(P, dtype=f), "tri": (i[:, None] < i[None, :]).astype(f), "ones": np.ones((P, P), f),
         "mhalf": np.full((P, 16), -0.5, f)}
    c["eps"] = np.full((P, 16), RMS_EPS, f)
    c["eps"][:, 15] = LN_EPS

    def all_rows(v):
        return np.ascontiguousarray(np.broadcast_to(np.asarray(v, f), (P,) + np.shape(v)))
    c["rev"] = all_rows(np.arange(PER, 0, -1))
    c["edges"] = all_rows(P * np.arange(NT))
    c["block_no"] = all_rows(np.arange(NB + 2))
    e = np.arange(NE)
    c["upto"] = all_rows(e[:, None] >= e[None, :])
    pos = np.arange(SEQ)
    rc = np.stack([pos // GRID_W, pos % GRID_W]).astype(f)
    for name, dim in (("rope_mla", ROPE), ("rope_gqa", HD)):
        half = dim // 2
        inv = (f(ROPE_BASE) ** (-(np.arange(0, half, 2, dtype=f) / f(half)))).astype(f)
        ang = (rc[:, :, None] * inv).astype(f).astype(np.float64)
        cos, sin = np.cos(ang).astype(f), np.sin(ang).astype(f)
        t = np.zeros((NT, P, 2, 2, 2, half // 2), f)
        t[:, :, 0] = 1.0
        for p in range(2):
            for h in range(2):
                t[CT:, :, 0, p, h] = cos[p].reshape(LT, P, -1)
                t[CT:, :, 1, p, h] = sin[p].reshape(LT, P, -1) * (-1 if h == 0 else 1)
        c[name] = np.ascontiguousarray(t.transpose(1, 0, 2, 3, 4, 5).reshape(P, NT, 2, dim))
    return c


def kernel(**inputs):
    import concourse.bacc as _bacc
    from concourse.bass_utils import run_bass_kernel_spmd as _run

    nc = _bacc.Bacc("TRN2", target_bir_lowering=False, num_devices=1)
    arrays, A, consts = {}, {}, {}
    for name in _INS:
        a = np.ascontiguousarray(inputs[name])
        arrays[f"in_{name}"] = a
        A[name] = nc.dram_tensor(f"in_{name}", a.shape, mybir.dt.from_np(a.dtype), kind="ExternalInput").ap()
    for name, a in constants().items():
        arrays[f"const_{name}"] = a
        consts[name] = nc.dram_tensor(f"const_{name}", a.shape, F32, kind="ExternalInput").ap()
    out = nc.dram_tensor("out_0", (1, SEQ, D), F32, kind="ExternalOutput").ap()
    backbone(nc, A, consts, out)
    r = _run(nc, [arrays], core_ids=[0])
    return r.results[0]["out_0"]
```

```python
import numpy as np
import concourse.bass as bass
from concourse import mybir
from contextlib import ExitStack, contextmanager

F32 = mybir.dt.float32
I32 = mybir.dt.int32
F32R = mybir.dt.float32r
ALU = mybir.AluOpType
ACT = mybir.ActivationFunctionType
AX = mybir.AxisListType

P = 128
D = 1024
SEQ = 1024
CTX = 256
DEPTH = 2
KC = D // P
CT = CTX // P
LT = SEQ // P
NT = CT + LT
GRID_W = 64
ROPE_BASE = 10000.0
RMS_EPS = 1e-6
LN_EPS = 1e-5
H_MLA, QLORA, KVLORA, NOPE, ROPE, VD = 8, 384, 256, 64, 32, 64
QK = NOPE + ROPE
MLA_SCALE = QK ** -0.5
H_GQA, H_KV, HD = 8, 2, 64
GQA_SCALE = HD ** -0.5
HEADS = H_MLA + H_GQA
Z_KR = QLORA + KVLORA
Z_G = Z_KR + ROPE
G_ALL = H_GQA + H_KV
Z_V = Z_G + G_ALL * HD
Z_ALL = Z_V + H_KV * HD
NGRP, PER, NE, TOPK, FF = 4, 8, 32, 2, 512
ALPHA = (2.0 * DEPTH) ** 0.25
BIG = 1.0e30


def n_blocks(tiles):
    return (tiles * P * TOPK + NE * (P - 1)) // P


NB = n_blocks(NT)
NBP = NB + NB % 2


class Chain:

    def __init__(self, eng, sem):
        self.eng, self.sem, self.base, self.n = eng, sem, 0, 0

    def start(self, base):
        self.base, self.n = base, 0

    def step(self, ins):
        ins.then_inc(self.sem, 1)
        self.n += 1
        return self.base + self.n

    def link(self, ins):
        self.eng.wait_ge(self.sem, self.step(ins) + 1)


@contextmanager
def semaphores(nc):
    got = []

    def new(name, start=1):
        got.append(nc.alloc_semaphore(name))
        if start:
            nc.sync.sem_inc(got[-1], start)
        return got[-1]

    yield new
    nc.clear_and_free_semaphores(got)
    nc.all_engine_barrier()



def modulation(nc, A, S):
    NW, BUF = 512, 3
    with ExitStack() as cx:
        new_semaphore = cx.enter_context(semaphores(nc))
        wt = cx.enter_context(nc.sbuf_tensor("ada_w", [P, BUF, KC, NW], F32))
        ccol = cx.enter_context(nc.sbuf_tensor("ada_c", [P, 2, KC], F32))
        scol = cx.enter_context(nc.sbuf_tensor("ada_silu", [P, KC, 2], F32))
        brow = cx.enter_context(nc.sbuf_tensor("ada_bias", [2, DEPTH * 6 * D], F32))
        row = cx.enter_context(nc.sbuf_tensor("ada_row", [2, DEPTH * 6 * D], F32))
        ps = cx.enter_context(nc.psum_tensor("ada_ps", [P, BUF, NW], F32))
        w_full = [new_semaphore(f"ada_w_full{u}") for u in range(BUF)]
        small = new_semaphore("ada_small_loaded")
        silu_done = new_semaphore("ada_silu_done")
        mm_done = new_semaphore("ada_mm_done")
        evac = new_semaphore("ada_evacuated")
        stored = new_semaphore("ada_stored")
        copied = new_semaphore("stream_copied")
        per = 6 * D // NW // BUF
        block = cx.enter_context(nc.Block())

        @block.sync
        def _(sp):
            for layer in range(DEPTH):
                w = A["w_ada"][layer].rearrange("(p a) n -> p a n", a=KC)
                with sp.Fori(0, per) as i:
                    for u in range(BUF):
                        if layer:
                            sp.wait_ge(mm_done, (i + layer * per - 1) * BUF + u + 2)
                            sp.dma_start(wt[:, u], w[:, :, bass.ds((i * BUF + u) * NW, NW)]).then_inc(w_full[u], 16)
                        else:
                            sp.wait_ge(mm_done, i * BUF + 1)
                            sp.dma_start(wt[:, u], w[:, :, bass.ds((i * BUF + u) * NW, NW)]).then_inc(w_full[u], 16)
            sp.wait_ge(evac, DEPTH * per * BUF + 1)
            sp.dma_start(S["ada"][:, :], row[:, :]).then_inc(stored, 16)
            sp.wait_ge(stored, 17)

        @block.scalar
        def _(act):
            act.dma_start(ccol[:, 0, :], A["c_ctx"].rearrange("(p a) -> p a", a=KC)).then_inc(small, 16)
            act.dma_start(ccol[:, 1, :], A["c"][0].rearrange("(p a) -> p a", a=KC)).then_inc(small, 16)
            act.dma_start(brow[:, :], A["b_ada"].rearrange("l n -> (l n)").partition_broadcast(2)).then_inc(small, 16)
            act.dma_start(S["x_s"][0:CTX, :], A["ctx"][0]).then_inc(copied, 16)
            act.dma_start(S["x_s"][CTX:CTX + SEQ, :], A["x"][0]).then_inc(copied, 16)
            act.wait_ge(small, 49)
            nc.scalar.activation(scol[:, :, :].rearrange("p a s -> p s a"), ccol[:, :, :], ACT.Silu).then_inc(silu_done, 1)
            act.wait_ge(copied, 33)

        @block.tensor
        def _(pe):
            pe.wait_ge(silu_done, 2)
            for layer in range(DEPTH):
                with pe.Fori(0, per) as i:
                    for u in range(BUF):
                        pe.wait_ge(w_full[u], (i + layer * per + 1) * 16 + 1)
                        if layer:
                            pe.wait_ge(evac, (i + layer * per - 1) * BUF + u + 2)
                        else:
                            pe.wait_ge(evac, i * BUF + 1)
                        for k in range(KC):
                            last = nc.tensor.matmul(ps[0:2, u, :], scol[:, k, :], wt[:, u, k, :],
                                                    start=(k == 0), stop=(k == KC - 1))
                        last.then_inc(mm_done, 1)

        @block.vector
        def _(dve):
            dve.wait_ge(small, 49)
            for layer in range(DEPTH):
                with dve.Fori(0, per) as i:
                    for u in range(BUF):
                        dve.wait_ge(mm_done, (i + layer * per) * BUF + u + 2)
                        cols = bass.ds((i * BUF + u) * NW + layer * 6 * D, NW)
                        nc.vector.tensor_tensor(row[:, cols], ps[0:2, u, :], brow[:, cols], ALU.add).then_inc(evac, 1)



def projections(nc, A, S, C, layer):
    last_layer = layer == DEPTH - 1
    ZW = Z_ALL // 3
    with ExitStack() as cx:
        new_semaphore = cx.enter_context(semaphores(nc))

        def sb(name, shape, dt=F32):
            return cx.enter_context(nc.sbuf_tensor(f"{name}{layer}", shape, dt))

        def sem(name, start=1):
            return new_semaphore(f"{name}{layer}", start)

        w_in = sb("w_in", [P, KC, Z_ALL])
        w_q = sb("w_q", [P, QLORA // P, H_MLA * QK])
        w_kv = sb("w_kv", [P, KVLORA // P, H_MLA * (NOPE + VD)])
        g_col = sb("g_col", [P, 5])
        g_row = sb("g_row", [P, G_ALL, HD])
        mod = sb("mod", [P, 2, 2, KC])
        modt = sb("modt", [P, NT, 2, KC])
        xt = sb("xt", [P, D])
        hT = sb("hT", [P, KC, P])
        z = sb("z", [P, Z_ALL])
        junk = sb("junk", [P, QLORA])
        sq = sb("sq", [P, G_ALL, HD])
        ms = sb("ms", [P, 2 + G_ALL])
        rstd = sb("rstd", [P, 2 + G_ALL])
        qa = sb("qa", [P, 5, P])
        qaT = sb("qaT", [P, 5, P])
        q_tok = sb("q_tok", [P, H_MLA + 1, QK])
        k_tok = sb("k_tok", [P, H_MLA, QK])
        gn = sb("gn", [P, G_ALL, HD])
        vg = sb("vg", [P, H_KV * HD])
        g_tok = sb("g_tok", [P, G_ALL, HD])
        r_a = sb("r_a", [P, G_ALL, HD])
        r_b = sb("r_b", [P, G_ALL, HD])
        gq2 = sb("gq2", [P, H_GQA, 2, HD], F32R)
        gk2 = sb("gk2", [P, 2, H_KV, 2, HD], F32R)
        qT = [sb(f"qT{n}", [QK, H_MLA, P], F32R) for n in range(2)]
        kT = [sb(f"kT{n}", [QK, H_MLA, P], F32R) for n in range(2)]
        gqT = sb("gqT", [P, H_GQA, P], F32R)
        gkT = sb("gkT", [P, 2 * H_KV, P], F32R)
        v = sb("v", [P, (H_MLA + H_KV) * VD])
        rope_mla = sb("rope_mla", [P, NT, 2, ROPE])
        rope_gqa = sb("rope_gqa", [P, NT, 2, HD])
        tp = [cx.enter_context(nc.psum_tensor(f"tp{b}_{layer}", [P, 4, P], F32)) for b in range(2)]
        zp = cx.enter_context(nc.psum_tensor(f"zp{layer}", [P, 3, 512], F32))
        up = cx.enter_context(nc.psum_tensor(f"up{layer}", [P, 3, 512], F32))

        w_loaded, x_loaded = sem("w_loaded"), sem("x_loaded")
        prep = sem("prep", 0)
        t_full, freed, hi_done = sem("t_full"), [sem("freed0"), sem("freed1")], sem("hi_done")
        z_full, z_out = sem("z_full"), sem("z_out")
        z_act, norm_in, norm_out, qa_ready = sem("z_act"), sem("norm_in"), sem("norm_out"), sem("qa_ready")
        up_full, up_act, up_dve = sem("up_full"), sem("up_act"), sem("up_dve")
        modt_ready, q_stored, eps_added = sem("modt_ready"), sem("q_stored"), sem("eps_added")
        g_hi, t_loaded = sem("g_hi"), sem("t_loaded")
        dve_step, act_step, pool_step = sem("dve_step"), sem("act_step"), sem("pool_step")
        block = cx.enter_context(nc.Block())

        PRE, A2, B1 = 8, 5, 16
        TG = 12
        NST = 7

        @block.sync
        def _(sp):
            def load_x(t):
                sp.dma_start(xt[:, :], S["x_s"].rearrange("(t p) n -> t p n", p=P)[bass.ds(t, 1)]
                             .rearrange("a p n -> p (a n)")).then_inc(x_loaded, 16)

            def store(t, ends=0):
                for b in range(2):
                    sp.wait_ge(freed[b], 1 + 6 * t + 6 - ends + 1)
                for n in range(2):
                    sp.dma_start(S["q_mla"][bass.ds(t, 1), n].rearrange("a p h n -> p (a h) n"),
                                 qT[n][:, :, :].bitcast(F32)).then_inc(q_stored, 16)
                    sp.dma_start(S["k_mla"][n, :, :, bass.ds(t * P, P)], kT[n][:, :, :].bitcast(F32)).then_inc(q_stored, 16)
                sp.dma_start(S["q_gqa"][bass.ds(t, 1)].rearrange("a p h n -> p (a h) n"), gqT[:, :, :].bitcast(F32)).then_inc(q_stored, 16)
                sp.dma_start(S["k_gqa"][:, :, bass.ds(t * P, P)], gkT[:, :, :].bitcast(F32)).then_inc(q_stored, 16)
                sp.dma_start(S["v_s"].rearrange("(t p) n -> t p n", p=P)[bass.ds(t, 1)]
                             .rearrange("a p n -> p (a n)"), v[:, :]).then_inc(q_stored, 16)

            w = A["w_in"][layer].rearrange("(a p) n -> p a n", p=P)
            load_x(0)
            sp.dma_start(rope_mla[:, :, :, :], C["dram"]["rope_mla"]).then_inc(t_loaded, 16)
            sp.dma_start(rope_gqa[:, :, :, :], C["dram"]["rope_gqa"]).then_inc(t_loaded, 16)
            sp.dma_start(w_in[:, :, :], w).then_inc(w_loaded, 16)
            sp.dma_start(w_q[:, :, :], A["w_q_b"][layer].rearrange("(a p) n -> p a n", p=P)).then_inc(w_loaded, 16)
            sp.dma_start(w_kv[:, :, :], A["w_kv_b"][layer].rearrange("(a p) n -> p a n", p=P)).then_inc(w_loaded, 16)
            sp.wait_ge(t_full, 3)
            load_x(1)
            store(0)
            with sp.Fori(2, NT) as t:
                sp.wait_ge(t_full, 2 + TG * (t - 2) + 3)
                load_x(t)
                store(t - 1)
            store(NT - 1, 1)
            sp.wait_ge(q_stored, 16 * NST * NT + 1)

        @block.gpsimd
        def _(pool):
            with nc.allow_non_contiguous_dma(reason="a few thousand column entries"):
                for s in range(2):
                    for n, part in enumerate((0, 1)):
                        o = layer * 6 * D + part * D
                        pool.dma_start(mod[:, s, n, :], S["ada"][s, o:o + D].rearrange("(a p) -> p a", p=P)).then_inc(prep, 16)
                pool.dma_start(g_col[:, 0:3], A["g_q_a"][layer].rearrange("(a p) -> p a", p=P)).then_inc(prep, 16)
                pool.dma_start(g_col[:, 3:5], A["g_kv_a"][layer].rearrange("(a p) -> p a", p=P)).then_inc(prep, 16)
            pool.dma_start(r_a[:, 0, :], A["g_gqa_q"][layer].partition_broadcast(P)).then_inc(prep, 16)
            pool.dma_start(r_a[:, 1, :], A["g_gqa_k"][layer].partition_broadcast(P)).then_inc(prep, 16)
            if layer == 0:
                nc.gpsimd.memset(C["zeros"][:, :], 0.0).then_inc(pool_step, 1)
                pool.wait_ge(pool_step, 2)
                pool.dma_start(S["xb"].rearrange("(b p) n -> p b n", p=P),
                               C["zeros"][:, :].unsqueeze(1).to_broadcast([P, NBP + 3, D])).then_inc(C["xb_zeroed"], 16)
            with pool.Fori(0, NT) as t:
                pool.wait_ge(norm_in, t + 2)
                pool.wait_ge(act_step, 2 * t + 3)
                nc.gpsimd.tensor_tensor(ms[:, :], ms[:, :], C["eps"][:, 0:2 + G_ALL], ALU.add).then_inc(eps_added, 1)
                pool.wait_ge(eps_added, t + 2)
                nc.gpsimd.tensor_tensor(rstd[:, :], ms[:, :], C["mhalf"][:, 0:2 + G_ALL], ALU.pow).then_inc(norm_out, 1)
            if layer == 0:
                pool.wait_ge(C["xb_zeroed"], 16)

        @block.scalar
        def _(act):
            def part_a1(t, g):
                act.wait_ge(t_full, g + 2)
                act.wait_ge(z_full, 3 * t + 1)
                for k in range(4):
                    ins = nc.scalar.activation(hT[:, k, :], tp[0][:, k, :], ACT.Identity,
                                               bias=modt[:, bass.ds(t, 1), 0, k:k + 1].rearrange("p a b -> p (a b)"),
                                               scale=modt[:, bass.ds(t, 1), 1, k:k + 1].rearrange("p a b -> p (a b)"))
                ins.then_inc(freed[0], 1)

            def part_a2(t):
                act.wait_ge(z_full, 3 * t + 2)
                nc.scalar.activation(z[:, 0:ZW], zp[:, 0, 0:ZW], ACT.Copy).then_inc(z_act, 1)
                act.wait_ge(z_act, t + 2)
                act.wait_ge(z_out, 2 * t + 2)
                nc.scalar.activation(junk[:, 0:QLORA], z[:, 0:QLORA], ACT.Square, scale=QLORA ** -0.5,
                                     accum_out=ms[:, 0:1]).then_inc(act_step, 1)
                act.wait_ge(act_step, 2 * t + 2)
                nc.scalar.activation(junk[:, 0:KVLORA], z[:, QLORA:Z_KR], ACT.Square, scale=KVLORA ** -0.5,
                                     accum_out=ms[:, 1:2]).then_inc(act_step, 1)
                act.wait_ge(norm_out, t + 2)
                nc.scalar.activation(qa[:, 0:3, :].rearrange("p a n -> p (a n)"), z[:, 0:QLORA], ACT.Copy,
                                     scale=rstd[:, 0:1])
                nc.scalar.activation(qa[:, 3:5, :].rearrange("p a n -> p (a n)"), z[:, QLORA:Z_KR], ACT.Copy,
                                     scale=rstd[:, 1:2]).then_inc(qa_ready, 1)

            def part_b1(t, g):
                act.wait_ge(t_full, g + 4)
                act.wait_ge(up_full, 4 * t + 1)
                nc.scalar.activation(qaT[:, 0:3, :], tp[0][:, 0:3, :], ACT.Copy).then_inc(freed[0], 1)
                for n in range(2):
                    act.wait_ge(up_full, 4 * t + n + 2)
                    nc.scalar.activation(q_tok[:, 4 * n:4 * n + 4, :], up[:, n, 0:4 * QK].rearrange("p (h d) -> p h d", h=4),
                                         ACT.Copy, scale=MLA_SCALE).then_inc(up_act, 1)
                act.wait_ge(up_full, 4 * t + 4)
                kv = up[:, 2, :].rearrange("p (h d) -> p h d", h=4)
                nc.scalar.activation(k_tok[:, 0:4, 0:NOPE], kv[:, :, 0:NOPE], ACT.Copy)
                act.wait_ge(q_stored, 16 * NST * t + 1)
                nc.scalar.activation(v[:, 0:4 * VD].rearrange("p (h d) -> p h d", h=4),
                                     kv[:, :, NOPE:NOPE + VD], ACT.Copy).then_inc(up_act, 1)
                act.wait_ge(dve_step, PRE + A2 + 6 + t * (A2 + B1) + 1)
                nc.scalar.activation(gq2[:, :, 0, :], g_tok[:, 0:H_GQA, :], ACT.Copy)
                nc.scalar.activation(gk2[:, 0, :, :, :], g_tok[:, H_GQA:G_ALL, :].unsqueeze(2).to_broadcast([P, H_KV, 2, HD]),
                                     ACT.Copy).then_inc(g_hi, 1)

            def part_b2(t, g):
                act.wait_ge(q_stored, 16 * NST * t + 1)
                for n, dst in enumerate((kT, kT, qT, qT)):
                    act.wait_ge(t_full, g + 5 + n + 1)
                    h0 = 4 * (n % 2)
                    nc.scalar.activation(dst[0][:, h0:h0 + 4, :], tp[n % 2][0:QK, :, :], ACT.Copy).then_inc(hi_done, 1)
                act.wait_ge(t_full, g + 10)
                nc.scalar.activation(gqT[:, 0:4, :], tp[0][:, :, :], ACT.Copy).then_inc(freed[0], 1)
                act.wait_ge(t_full, g + 12)
                nc.scalar.activation(gkT[:, 0:2, :], tp[0][:, 0:2, :], ACT.Copy).then_inc(freed[0], 1)

            act.wait_ge(prep, 128)
            nc.scalar.activation(modt[:, 0:CT], mod[:, 0:1].to_broadcast([P, CT, 2, KC]), ACT.Copy)
            nc.scalar.activation(modt[:, CT:NT], mod[:, 1:2].to_broadcast([P, LT, 2, KC]), ACT.Copy).then_inc(modt_ready, 1)
            act.wait_ge(dve_step, PRE + 1)
            part_a1(0, 0)
            with act.Fori(1, NT) as t:
                g = 2 + TG * (t - 1)
                part_a1(t, g)
                part_a2(t - 1)
                part_b1(t - 1, g)
                part_b2(t - 1, g)
            part_a2(NT - 1)
            part_b1(NT - 1, 2 + TG * (NT - 1) - 2)
            part_b2(NT - 1, 2 + TG * (NT - 1) - 2)

        @block.vector
        def _(dve):
            ch = Chain(dve, dve_step)

            def turn(dst, src, heads, half, table, tile):
                w = 4 * half
                cos = table[:, bass.ds(tile, 1), 0, :].to_broadcast([P, heads, w])
                sin = table[:, bass.ds(tile, 1), 1, :].to_broadcast([P, heads, w])
                a, b = r_a[:, 0:heads, 0:w], r_b[:, 0:heads, 0:w]
                ch.step(nc.vector.tensor_tensor(a, src, cos, ALU.mult))
                for part in range(2):
                    for h in range(2):
                        o, i = part * 2 * half + h * half, part * 2 * half + (1 - h) * half
                        last = ch.step(nc.vector.tensor_tensor(b[:, :, o:o + half], src[:, :, i:i + half],
                                                               sin[:, :, o:o + half], ALU.mult))
                dve.wait_ge(dve_step, last + 1)
                ch.link(nc.vector.tensor_tensor(dst, a, b, ALU.add))

            def part_a1(t, g):
                dve.wait_ge(t_full, g + 3)
                dve.wait_ge(z_full, 3 * t + 1)
                for k in range(4, KC):
                    ins = nc.vector.tensor_scalar(hT[:, k, :], tp[1][:, k - 4, :],
                                                  modt[:, bass.ds(t, 1), 1, k:k + 1].rearrange("p a b -> p (a b)"),
                                                  modt[:, bass.ds(t, 1), 0, k:k + 1].rearrange("p a b -> p (a b)"),
                                                  ALU.mult, ALU.add)
                ins.then_inc(freed[1], 1)

            def part_b1(t, g):
                dve.wait_ge(t_full, g + 5)
                dve.wait_ge(up_full, 4 * t + 1)
                nc.vector.tensor_copy(qaT[:, 3:5, :], tp[1][:, 0:2, :]).then_inc(freed[1], 1)
                turn(g_tok[:, :, :], gn[:, :, :], G_ALL, HD // 4, rope_gqa, t)
                dve.wait_ge(up_act, 3 * t + 3)
                r = q_tok[:, :, NOPE:QK]
                turn(r, r, H_MLA + 1, ROPE // 4, rope_mla, t)
                dve.wait_ge(up_full, 4 * t + 5)
                kv = up[:, 0, :].rearrange("p (h d) -> p h d", h=4)
                nc.vector.tensor_copy(k_tok[:, 4:8, 0:NOPE], kv[:, :, 0:NOPE])
                dve.wait_ge(q_stored, 16 * NST * t + 1)
                nc.vector.tensor_copy(v[:, 4 * VD:8 * VD].rearrange("p (h d) -> p h d", h=4),
                                      kv[:, :, NOPE:NOPE + VD]).then_inc(up_dve, 1)
                ch.step(nc.vector.tensor_copy(v[:, 8 * VD:10 * VD], vg[:, :]))
                dve.wait_ge(g_hi, t + 2)
                ch.step(nc.vector.tensor_tensor(gq2[:, :, 1, :], g_tok[:, 0:H_GQA, :], gq2[:, :, 0, :].bitcast(F32), ALU.subtract))
                ch.step(nc.vector.tensor_tensor(gk2[:, 1, :, :, :], g_tok[:, H_GQA:G_ALL, :].unsqueeze(2).to_broadcast([P, H_KV, 2, HD]),
                                                gk2[:, 0, :, :, :].bitcast(F32), ALU.subtract))
                ch.link(nc.vector.tensor_copy(k_tok[:, :, NOPE:QK],
                                              q_tok[:, H_MLA:H_MLA + 1, NOPE:QK].to_broadcast([P, H_MLA, ROPE])))

            def part_a2(t):
                for n in (1, 2):
                    dve.wait_ge(z_full, 3 * t + n + 2)
                    nc.vector.tensor_copy(z[:, n * ZW:(n + 1) * ZW], zp[:, n, 0:ZW]).then_inc(z_out, 1)
                dve.wait_ge(z_out, 2 * t + 3)
                zg = z[:, Z_G:Z_V].rearrange("p (h d) -> p h d", d=HD)
                ch.link(nc.vector.scalar_tensor_tensor(sq[:, :, :], zg, 1.0 / HD, zg, ALU.mult, ALU.mult))
                nc.vector.tensor_reduce(ms[:, 2:2 + G_ALL], sq[:, :, :], AX.X, ALU.add).then_inc(norm_in, 1)
                ch.step(nc.vector.tensor_copy(vg[:, :], z[:, Z_V:Z_ALL]))
                ch.step(nc.vector.tensor_copy(q_tok[:, H_MLA, NOPE:QK], z[:, Z_KR:Z_G]))
                dve.wait_ge(norm_out, t + 2)
                ch.link(nc.vector.tensor_tensor(gn[:, :, :], zg,
                                                rstd[:, 2:2 + G_ALL].unsqueeze(2).to_broadcast([P, G_ALL, HD]), ALU.mult))
                ch.link(nc.vector.tensor_tensor(gn[:, :, :], gn[:, :, :], g_row[:, :, :], ALU.mult))

            def part_b2(t, g):
                dve.wait_ge(q_stored, 16 * NST * t + 1)
                for n, dst in enumerate((kT, kT, qT, qT)):
                    h0 = 4 * (n % 2)
                    dve.wait_ge(hi_done, 4 * t + n + 2)
                    nc.vector.tensor_tensor(dst[1][:, h0:h0 + 4, :], tp[n % 2][0:QK, :, :],
                                            dst[0][:, h0:h0 + 4, :].bitcast(F32), ALU.subtract).then_inc(freed[n % 2], 1)
                dve.wait_ge(t_full, g + 11)
                nc.vector.tensor_copy(gqT[:, 4:8, :], tp[1][:, :, :]).then_inc(freed[1], 1)
                dve.wait_ge(t_full, g + 13)
                nc.vector.tensor_copy(gkT[:, 2:4, :], tp[1][:, 0:2, :]).then_inc(freed[1], 1)

            dve.wait_ge(prep, 128)
            dve.wait_ge(modt_ready, 2)
            ch.step(nc.vector.tensor_scalar(modt[:, :, 1, :], modt[:, :, 1, :], 1.0, None, ALU.add))
            ch.step(nc.vector.tensor_scalar(g_row[:, 0:H_GQA, :], r_a[:, 0:1, :].to_broadcast([P, H_GQA, HD]),
                                            GQA_SCALE, None, ALU.mult))
            ch.step(nc.vector.tensor_copy(g_row[:, H_GQA:G_ALL, :], r_a[:, 1:2, :].to_broadcast([P, H_KV, HD])))
            dve.wait_ge(w_loaded, 49)
            dve.wait_ge(t_loaded, 33)
            for k in range(3):
                ch.step(nc.vector.tensor_scalar(w_q[:, k, :], w_q[:, k, :], g_col[:, k:k + 1], None, ALU.mult))
            for k in range(2):
                ch.step(nc.vector.tensor_scalar(w_kv[:, k, :], w_kv[:, k, :], g_col[:, 3 + k:4 + k], None, ALU.mult))
            assert ch.n == PRE
            part_a1(0, 0)
            with dve.Fori(1, NT) as t:
                g = 2 + TG * (t - 1)
                ch.start((t - 1) * (A2 + B1) + PRE)
                part_a1(t, g)
                part_a2(t - 1)
                assert ch.n == A2
                part_b1(t - 1, g)
                assert ch.n == A2 + B1
                part_b2(t - 1, g)
            ch.start(PRE + (NT - 1) * (A2 + B1))
            part_a2(NT - 1)
            part_b1(NT - 1, 2 + TG * (NT - 1) - 2)
            part_b2(NT - 1, 2 + TG * (NT - 1) - 2)

        @block.tensor
        def _(pe):
            ident = C["ident"]

            def bank_free(b, n):
                pe.wait_ge(freed[b], n + 1)

            def part_x(t, taken):
                pe.wait_ge(x_loaded, 16 * (t + 1) + 1)
                for b in range(2):
                    bank_free(b, taken)
                    for k in range(4):
                        ins = nc.tensor.transpose(tp[b][:, k, :], xt[:, bass.ts(4 * b + k, P)], ident[:, :])
                    ins.then_inc(t_full, 1)

            def groups(jobs, taken, between=None):
                for n, job in enumerate(jobs):
                    b = n % 2
                    bank_free(b, taken + n // 2)
                    for k, (src, rows) in enumerate(job):
                        ins = nc.tensor.transpose(tp[b][0:rows, k, :], src, ident[:, :])
                    ins.then_inc(t_full, 1)
                    if between:
                        between(n)

            def part_z(t, n, taken=None, chunks=range(KC)):
                if taken is not None:
                    bank_free(0, taken + 1)
                    bank_free(1, taken + 1)
                if 0 in chunks:
                    if n == 0:
                        pe.wait_ge(z_act, t + 1)
                    else:
                        pe.wait_ge(z_out, 2 * t + 1)
                for k in chunks:
                    ins = nc.tensor.matmul(zp[:, n, 0:ZW], hT[:, k, :], w_in[:, k, n * ZW:(n + 1) * ZW],
                                           start=(k == 0), stop=(k == KC - 1))
                if KC - 1 in chunks:
                    ins.then_inc(z_full, 1)

            def part_b1(t, taken):
                pe.wait_ge(qa_ready, t + 2)
                groups([[(qa[:, k, :], P) for k in range(3)], [(qa[:, k, :], P) for k in (3, 4)]], taken)

            def part_up(t, taken):
                bank_free(0, taken + 1)
                HW = 4 * QK
                for n in range(2):
                    if n == 0:
                        pe.wait_ge(up_act, 3 * t + 1)
                        pe.wait_ge(up_dve, t + 1)
                    for k in range(3):
                        ins = nc.tensor.matmul(up[:, n, 0:HW], qaT[:, k, :], w_q[:, k, n * HW:(n + 1) * HW],
                                               start=(k == 0), stop=(k == 2))
                    ins.then_inc(up_full, 1)
                bank_free(1, taken + 1)
                for n, b in ((0, 2), (1, 0)):
                    if n == 1:
                        pe.wait_ge(up_act, 3 * t + 2)
                    for k in range(2):
                        ins = nc.tensor.matmul(up[:, b, :], qaT[:, 3 + k, :], w_kv[:, k, n * 512:(n + 1) * 512],
                                               start=(k == 0), stop=(k == 1))
                    ins.then_inc(up_full, 1)

            def part_heads(t, taken, between=None):
                pe.wait_ge(dve_step, PRE + A2 + B1 + t * (A2 + B1) + 1)
                pe.wait_ge(up_act, 3 * t + 4)
                pe.wait_ge(up_dve, t + 2)
                gg = gq2[:, :, :, :].bitcast(F32).rearrange("p h a d -> p (h a d)")
                kk = gk2[:, :, :, :, :].bitcast(F32).rearrange("p a h b d -> p (a h b d)")
                groups([[(k_tok[:, h, :], QK) for h in range(4)], [(k_tok[:, h, :], QK) for h in range(4, 8)],
                           [(q_tok[:, h, :], QK) for h in range(4)], [(q_tok[:, h, :], QK) for h in range(4, 8)],
                           [(gg[:, bass.ts(j, P)], P) for j in range(4)], [(gg[:, bass.ts(j, P)], P) for j in range(4, 8)],
                           [(kk[:, bass.ts(j, P)], P) for j in range(2)], [(kk[:, bass.ts(j, P)], P) for j in range(2, 4)]], taken, between)

            pe.wait_ge(dve_step, PRE + 1)
            pe.wait_ge(w_loaded, 49)
            part_x(0, 0)
            for n in range(3):
                part_z(0, n, 0 if n == 0 else None)
            with pe.Fori(1, NT) as t:
                taken = 1 + 6 * (t - 1)
                part_x(t, taken)
                part_z(t, 0, taken)
                part_b1(t - 1, taken + 1)
                part_up(t - 1, taken + 1)
                part_z(t, 1)
                part_heads(t - 1, taken + 2, lambda k: part_z(t, 2, chunks=[k]))
            taken = 1 + 6 * (NT - 1)
            part_b1(NT - 1, taken)
            part_up(NT - 1, taken)
            part_heads(NT - 1, taken + 1)



def load_keys_values(nc, S, KV, sp):
    for j in range(H_MLA // 2):
        for n in range(2):
            sp.dma_start(KV["k_mla"][n][:, 2 * j:2 * j + 2, :].bitcast(F32),
                         S["k_mla"][n, :, 2 * j:2 * j + 2, :]).then_inc(KV["k_loaded"][j], 16)
        if j == 0:
            sp.dma_start(KV["v"][:, :, :], S["v_s"].rearrange("(t p) n -> p t n", p=P)).then_inc(KV["v_loaded"], 16)
    sp.dma_start(KV["k_gqa"][:, :, :].bitcast(F32), S["k_gqa"]).then_inc(KV["k_loaded"][H_MLA // 2], 16)


def attention(nc, S, C, KV, layer, tiles, kb, name):
    first, last_tile = tiles
    turns = (last_tile - first) // 2
    UNITS, STEPS = HEADS // 2, 2 * HEADS
    GRP = [(0, 4), (4, 7), (7, 10)] if kb == 10 else [(0, kb)]
    assert GRP[-1][1] == kb
    NG = len(GRP)
    PIECES = [(a, min(a + 512, kb * P)) for a in range(0, kb * P, 512)]
    SHARE = [range(kb * i // 4, kb * (i + 1) // 4) for i in range(4)]
    with ExitStack() as cx:
        new_semaphore = cx.enter_context(semaphores(nc))

        def sb(n, shape, dt=F32):
            return cx.enter_context(nc.sbuf_tensor(f"{n}_{name}{layer}", shape, dt))

        def sem(n, start=1):
            return new_semaphore(f"{n}_{name}{layer}", start)

        qm = [sb(f"qm{n}", [QK, 2, H_MLA, P], F32R) for n in range(2)]
        qg = sb("qg", [P, 2, H_GQA, P], F32R)
        pr = sb("pr", [P, 2, kb * P])
        pt = sb("pt", [P, 2, kb, 2, 2 * P])
        nmax = sb("nmax", [P, 2])
        rsum = sb("rsum", [P, 8])
        rinv = sb("rinv", [P, 4])
        diag = sb("diag", [P, 4, P])
        ot = sb("ot", [P, 2, P])
        sc = cx.enter_context(nc.psum_tensor(f"sc_{name}{layer}", [P, 2, 1536], F32))
        tp = cx.enter_context(nc.psum_tensor(f"tp_{name}{layer}", [P, 4, P], F32))
        op = cx.enter_context(nc.psum_tensor(f"op_{name}{layer}", [P, 2, 2 * P], F32))
        qm_loaded, qg_loaded, o_stored, o_left = sem("qm_loaded"), sem("qg_loaded"), sem("o_stored", 0), sem("o_left")
        s_full, max_done, exp_done = sem("s_full"), sem("max_done"), sem("exp_done")
        t_full, t_dve, t_act = sem("t_full"), sem("t_dve"), sem("t_act")
        inv_done, diag_done = sem("inv_done"), sem("diag_done")
        v_done, r_full, r_out, o_out = sem("v_done"), sem("r_full"), sem("r_out"), sem("o_out")
        rb = sb("rb", [P, 2 * P])
        block = cx.enter_context(nc.Block())
        N_DVE = min(NG, 2)

        def place(n):
            return n // 4, n % 4 // 2, n % 2

        @block.sync
        def _(sp):
            def q_rows(t, n):
                return S["q_mla"][bass.ds(2 * t + first, 2), n].rearrange("a p h n -> p a h n")

            def body(t):
                if not isinstance(t, int):
                    sp.wait_ge(s_full, STEPS * (t - 1) + 2 * H_MLA + 1)
                for n in range(2):
                    for a in range(2):
                        sp.dma_start(qm[n][:, a].bitcast(F32), S["q_mla"][bass.ds(2 * t + (first + a), 1), n]
                                     .rearrange("a p h n -> p (a h) n")).then_inc(qm_loaded, 16)
                if not isinstance(t, int):
                    sp.wait_ge(s_full, STEPS * t + 1)
                for a in range(2):
                    sp.dma_start(qg[:, a].bitcast(F32), S["q_gqa"][bass.ds(2 * t + (first + a), 1)]
                                 .rearrange("a p h n -> p (a h) n")).then_inc(qg_loaded, 16)
                if isinstance(t, int) and KV["fresh"]:
                    load_keys_values(nc, S, KV, sp)

            body(0)
            if turns > 1:
                with sp.Fori(1, turns) as t:
                    body(t)

        @block.tensor
        def _(pe):
            def scores(t, n, pieces):
                unit, hh, a = place(n)
                h = 2 * unit + hh
                if pieces[0] == 0:
                    if n % 4 == 0:
                        if h < H_MLA:
                            pe.wait_ge(KV["k_loaded"][unit], 33)
                        if h == 0:
                            pe.wait_ge(qm_loaded, 64 * (t + 1) + 1)
                        if h == H_MLA:
                            pe.wait_ge(KV["k_loaded"][H_MLA // 2], 17)
                            pe.wait_ge(qg_loaded, 32 * (t + 1) + 1)
                    pe.wait_ge(exp_done, STEPS * t + max(n - 1, 0) + 1)
                if h < H_MLA:
                    pairs = [(qm[x][:, a, h, :], KV["k_mla"][y][:, h, :]) for x, y in ((0, 0), (0, 1), (1, 0))]
                else:
                    g = h - H_MLA
                    pairs = [(qg[:, a, g, :], KV["k_gqa"][:, x * H_KV + g // (H_GQA // H_KV), :]) for x in range(2)]
                for p in pieces:
                    lo, hi = PIECES[p]
                    for m, (q, k) in enumerate(pairs):
                        ins = nc.tensor.matmul(sc[:, n % 2, lo:hi], q, k[:, lo:hi], start=(m == 0), stop=(m == len(pairs) - 1))
                if pieces[-1] == len(PIECES) - 1:
                    ins.then_inc(s_full, 1)

            def transposes(t, n, g):
                if g == 0:
                    pe.wait_ge(exp_done, STEPS * t + n + 2)
                    pe.wait_ge(t_dve, N_DVE * (STEPS * t + n) + 1)
                elif g == 1:
                    pe.wait_ge(t_act, STEPS * t + n + 2)
                else:
                    pe.wait_ge(t_dve, N_DVE * (STEPS * t + n) + g)
                lo, hi = GRP[g]
                for k in range(lo, hi):
                    ins = nc.tensor.transpose(tp[:, k - lo, :], pr[:, n % 2, k * P:(k + 1) * P], C["ident"][:, :])
                ins.then_inc(t_full, 1)

            def values(t, unit, blocks):
                if 0 in blocks:
                    if unit == 0:
                        pe.wait_ge(KV["v_loaded"], 17)
                    pe.wait_ge(t_dve, N_DVE * (STEPS * t + 4 * unit + 4) + 1)
                    if NG == 3:
                        pe.wait_ge(t_act, STEPS * t + 4 * unit + 5)
                    pe.wait_ge(o_out, UNITS * t + unit + 1)
                for k in blocks:
                    for hh in range(2):
                        h = 2 * unit + hh
                        col = h if h < H_MLA else H_MLA + (h - H_MLA) // (H_GQA // H_KV)
                        ins = nc.tensor.matmul(op[VD * hh:VD * hh + VD, 0, :], KV["v"][:, k, col * VD:(col + 1) * VD],
                                               pt[:, unit % 2, k, hh, :], start=(k == 0), stop=(k == kb - 1))
                if kb - 1 in blocks:
                    ins.then_inc(v_done, 1)

            def sums(t, unit):
                pe.wait_ge(diag_done, UNITS * t + unit + 2)
                for a in range(2):
                    for hh in range(2):
                        ins = nc.tensor.matmul(op[VD * hh:VD * hh + VD, 1, a * P:(a + 1) * P], C["ones"][:, 0:VD],
                                               diag[:, 2 * hh + a, :], start=True, stop=True)
                ins.then_inc(r_full, 1)

            with pe.Fori(0, turns) as t:
                every = list(range(len(PIECES)))
                scores(t, 0, every)
                scores(t, 1, every)
                for n in range(STEPS):
                    for i in range(3):
                        if i < NG:
                            transposes(t, n, i)
                        if n + 2 < STEPS and i < len(PIECES):
                            scores(t, n + 2, [i])
                    if n >= 4:
                        if SHARE[n % 4]:
                            values(t, n // 4 - 1, SHARE[n % 4])
                        if n % 4 == 3:
                            sums(t, n // 4 - 1)
                values(t, UNITS - 1, range(kb))
                sums(t, UNITS - 1)

        @block.scalar
        def _(act):
            def exponential(t, n):
                act.wait_ge(max_done, STEPS * t + n + 2)
                act.wait_ge(t_full, NG * (STEPS * t + max(n - 1, 0)) + 1)
                act.wait_ge(inv_done, STEPS * t + max(n - 7, 0) + 1)
                nc.scalar.activation(pr[:, n % 2, :], sc[:, n % 2, 0:kb * P], ACT.Exp, bias=nmax[:, n % 2:n % 2 + 1],
                                     accum_out=rsum[:, n % 8:n % 8 + 1]).then_inc(exp_done, 1)

            def spread(t, unit):
                act.wait_ge(r_full, UNITS * t + unit + 2)
                act.wait_ge(o_out, UNITS * t + unit + 1)
                nc.scalar.activation(rb[:, :], op[:, 1, :], ACT.Copy).then_inc(r_out, 1)

            with act.Fori(0, turns) as t:
                exponential(t, 0)
                for n in range(STEPS):
                    if NG == 3:
                        unit, hh, a = place(n)
                        act.wait_ge(t_full, NG * (STEPS * t + n) + 2)
                        act.wait_ge(v_done, UNITS * t + max(unit - 1, 0) + 1)
                        lo, hi = GRP[0]
                        nc.scalar.activation(pt[:, unit % 2, lo:hi, hh, a * P:(a + 1) * P], tp[:, 0:hi - lo, :],
                                             ACT.Copy).then_inc(t_act, 1)
                    if n + 1 < STEPS:
                        exponential(t, n + 1)
                    if n % 4 == 0 and n >= 8:
                        spread(t, n // 4 - 2)
                for unit in (UNITS - 2, UNITS - 1):
                    spread(t, unit)

        @block.vector
        def _(dve):
            def maximum(t, n):
                dve.wait_ge(s_full, STEPS * t + n + 2)
                dve.wait_ge(exp_done, STEPS * t + max(n - 1, 0) + 1)
                nc.vector.tensor_reduce(nmax[:, n % 2:n % 2 + 1], sc[:, n % 2, 0:kb * P], AX.X, ALU.max,
                                        negate=True).then_inc(max_done, 1)

            def take(t, n, g):
                unit, hh, a = place(n)
                dve.wait_ge(t_full, NG * (STEPS * t + n) + g + 2)
                dve.wait_ge(v_done, UNITS * t + max(unit - 1, 0) + 1)
                lo, hi = GRP[g]
                nc.vector.tensor_copy(pt[:, unit % 2, lo:hi, hh, a * P:(a + 1) * P], tp[:, 0:hi - lo, :]).then_inc(t_dve, 1)

            def diagonals(t, unit):
                dve.wait_ge(exp_done, STEPS * t + 4 * unit + 5)
                for i in range(4):
                    c = (4 * unit + i) % 8
                    nc.vector.reciprocal(rinv[:, i:i + 1], rsum[:, c:c + 1]).then_inc(inv_done, 1)
                dve.wait_ge(inv_done, STEPS * t + 4 * unit + 5)
                dve.wait_ge(r_full, UNITS * t + unit + 1)
                for i in range(4):
                    ins = nc.vector.tensor_scalar(diag[:, i, :], C["ident"][:, :], rinv[:, i:i + 1], None, ALU.mult)
                ins.then_inc(diag_done, 1)

            def output(t, unit):
                dve.wait_ge(v_done, UNITS * t + unit + 2)
                dve.wait_ge(r_out, UNITS * t + unit + 2)
                dve.wait_ge(o_left, UNITS * t + unit + 1)
                nc.vector.tensor_tensor(ot[:, :, :], op[:, 0, :].rearrange("p (a n) -> p a n", a=2),
                                        rb[:, :].rearrange("p (a n) -> p a n", a=2), ALU.mult).then_inc(o_out, 1)

            with dve.Fori(0, turns) as t:
                maximum(t, 0)
                for n in range(STEPS):
                    if n + 1 < STEPS:
                        maximum(t, n + 1)
                    take(t, n, 1 if NG == 3 else 0)
                    if n % 4 == 0 and n >= 8:
                        output(t, n // 4 - 2)
                    if NG == 3:
                        take(t, n, 2)
                    if n % 4 == 2 and n >= 4:
                        diagonals(t, n // 4 - 1)
                output(t, UNITS - 2)
                diagonals(t, UNITS - 1)
                output(t, UNITS - 1)

        @block.gpsimd
        def _(pool):
            with pool.Fori(0, turns) as t:
                for unit in range(UNITS):
                    pool.wait_ge(o_out, UNITS * t + unit + 2)
                    for a in range(2):
                        pool.dma_start(S["o_s"][bass.ds(2 * t + (first + a), 1), :, unit, :].rearrange("a p n -> p (a n)"),
                                       ot[:, a, :]).then_inc(o_stored, 16)
                    pool.wait_ge(o_stored, 32 * (UNITS * t + unit + 1))
                    pool.sem_inc(o_left, 1)



def norm_steps(nc, dve, ch, u, stats, mv, rs_wait, gain, bias, out, filler):
    for n in range(2):
        ch.step(nc.vector.bn_stats(stats[:, n, :], u[:, n * 512:(n + 1) * 512]))
    dve.wait_ge(ch.sem, ch.base + ch.n + 1)
    nc.vector.memset(filler, 0.0)
    rstd = rs_wait(nc.vector.bn_aggr(mv[:, :], stats[:, :, :]))
    ch.link(nc.vector.tensor_scalar(u[:, :], u[:, :], mv[:, 0:1], rstd, ALU.subtract, ALU.mult))
    ch.link(nc.vector.tensor_tensor(u[:, :], u[:, :], gain, ALU.mult))
    return nc.vector.tensor_tensor(out, u[:, :], bias, ALU.add)


def pool_rstd(nc, pool, C, mv, veps, rstd, mv_ready, eps_done, rstd_ready, t):
    pool.wait_ge(mv_ready, t + 2)
    nc.gpsimd.tensor_tensor(veps[:, :], mv[:, 1:2], C["eps"][:, 15:16], ALU.add).then_inc(eps_done, 1)
    pool.wait_ge(eps_done, t + 2)
    nc.gpsimd.tensor_tensor(rstd[:, :], veps[:, :], C["mhalf"][:, 0:1], ALU.pow).then_inc(rstd_ready, 1)



def mix_and_route(nc, A, S, C, LG, layer, stream):
    first, end = (0, CT) if stream == 0 else (CT, NT)
    n_tiles = end - first
    NR = NGRP + NE
    name = f"{'ctx' if stream == 0 else 'lat'}{layer}"
    with ExitStack() as cx:
        new_semaphore = cx.enter_context(semaphores(nc))

        def sb(n, shape):
            return cx.enter_context(nc.sbuf_tensor(f"mr_{n}_{name}", shape, F32))

        def sem(n, start=1):
            return new_semaphore(f"mr_{n}_{name}", start)

        w_o = sb("w_o", [P, KC, D])
        w_r = sb("w_r", [P, KC, NR])
        b_r = sb("b_r", [P, NR])
        bc = sb("bc", [P, 5, D])
        ot = sb("ot", [P, KC, P])
        xt = sb("xt", [P, D])
        oT = sb("oT", [P, KC, P])
        u = sb("u", [P, D])
        x1 = sb("x1", [P, D])
        h = sb("h", [P, D])
        hT = sb("hT", [P, KC, P])
        stats = sb("stats", [P, 2, 6])
        mv = sb("mv", [P, 2])
        veps = sb("veps", [P, 1])
        rstd = sb("rstd", [P, 1])
        filler = sb("filler", [P, 1])
        tp = [cx.enter_context(nc.psum_tensor(f"mr_tp{b}_{name}", [P, 4, P], F32)) for b in range(2)]
        mp = cx.enter_context(nc.psum_tensor(f"mr_mp_{name}", [P, D], F32))
        rp = cx.enter_context(nc.psum_tensor(f"mr_rp_{name}", [P, 512], F32))
        w_loaded, v_loaded, o_loaded, x_loaded = sem("w_loaded"), sem("v_loaded", 0), sem("o_loaded"), sem("x_loaded")
        t_full, t_act, t_dve = sem("t_full"), sem("t_act"), sem("t_dve")
        o_taken = sem("o_taken")
        mix_full, r_full, steps = sem("mix_full"), sem("r_full"), sem("steps")
        mv_ready, eps_done, rstd_ready = sem("mv_ready"), sem("eps_done"), sem("rstd_ready")
        x1_ready, h_ready, out_stored = sem("x1_ready"), sem("h_ready"), sem("out_stored")
        block = cx.enter_context(nc.Block())
        STEPS = 9

        def row(ap, t):
            return ap.rearrange("(t p) n -> t p n", p=P)[bass.ds(t + first, 1)].rearrange("a p n -> p (a n)")

        @block.sync
        def _(sp):
            def load(t):
                sp.dma_start(ot[:, :, :], S["o_s"][bass.ds(t + first, 1)].rearrange("a p c n -> p (a c) n")).then_inc(o_loaded, 16)
            load(0)
            sp.dma_start(w_o[:, :, :], A["w_o"][layer].rearrange("(a p) n -> p a n", p=P)).then_inc(w_loaded, 16)
            with sp.Fori(1, n_tiles) as t:
                sp.wait_ge(o_taken, t + 1)
                load(t)

        @block.gpsimd
        def _(pool):
            for n, part in enumerate((2, 3, 4)):
                c0 = layer * 6 * D + part * D
                pool.dma_start(bc[:, n, :], S["ada"][stream, c0:c0 + D].partition_broadcast(P)).then_inc(v_loaded, 16)
            pool.dma_start(bc[:, 3, :], A["ln1_g"][layer].partition_broadcast(P)).then_inc(v_loaded, 16)
            pool.dma_start(bc[:, 4, :], A["ln1_b"][layer].partition_broadcast(P)).then_inc(v_loaded, 16)
            pool.dma_start(w_r[:, :, 0:NGRP], A["w_router_grp"][layer].rearrange("(a p) n -> p a n", p=P)).then_inc(v_loaded, 16)
            pool.dma_start(w_r[:, :, NGRP:NR], A["w_router_exp"][layer].rearrange("(a p) n -> p a n", p=P)).then_inc(v_loaded, 16)
            pool.dma_start(b_r[:, 0:NGRP], A["b_router_grp"][layer].partition_broadcast(P)).then_inc(v_loaded, 16)
            pool.dma_start(b_r[:, NGRP:NR], A["b_router_exp"][layer].partition_broadcast(P)).then_inc(v_loaded, 16)
            with pool.Fori(0, n_tiles) as t:
                pool_rstd(nc, pool, C, mv, veps, rstd, mv_ready, eps_done, rstd_ready, t)

        @block.scalar
        def _(act):
            def take_o(t):
                act.wait_ge(o_loaded, 16 * (t + 1) + 1)
                act.wait_ge(mix_full, 2 * t + 1)
                nc.scalar.activation(oT[:, :, :], ot[:, :, :], ACT.Copy).then_inc(o_taken, 1)

            def take_h(t):
                act.wait_ge(t_full, 2 * t + 2)
                nc.scalar.activation(hT[:, 0:4, :], tp[0][:, :, :], ACT.Copy).then_inc(t_act, 1)

            def load_x(t):
                act.dma_start(xt[:, :], row(S["x_s"], t)).then_inc(x_loaded, 16)

            def store(t):
                act.wait_ge(x1_ready, t + 2)
                act.dma_start(row(S["x_s"], t), x1[:, :]).then_inc(out_stored, 16)
                act.wait_ge(h_ready, t + 2)
                act.dma_start(row(S["h_s"], t), h[:, :]).then_inc(out_stored, 16)

            load_x(0)
            take_o(0)
            with act.Fori(1, n_tiles) as t:
                take_o(t)
                act.wait_ge(x1_ready, t + 1)
                load_x(t)
                store(t - 1)
                take_h(t - 1)
            store(n_tiles - 1)
            take_h(n_tiles - 1)
            act.wait_ge(out_stored, 32 * n_tiles + 1)

        @block.tensor
        def _(pe):
            def groups(src, t_taken):
                for b in range(2):
                    pe.wait_ge(t_act if b == 0 else t_dve, t_taken + 1)
                    for k in range(4):
                        ins = nc.tensor.transpose(tp[b][:, k, :], src[:, bass.ts(4 * b + k, P)], C["ident"][:, :])
                    ins.then_inc(t_full, 1)

            def mix(t):
                pe.wait_ge(o_taken, t + 2)
                if not (isinstance(t, int) and t == 0):
                    pe.wait_ge(steps, STEPS * (t - 1) + 4)
                for n in range(2):
                    for k in range(KC):
                        ins = nc.tensor.matmul(mp[:, n * 512:(n + 1) * 512], oT[:, k, :], w_o[:, k, n * 512:(n + 1) * 512],
                                               start=(k == 0), stop=(k == KC - 1))
                    ins.then_inc(mix_full, 1)

            def route(t, taken):
                pe.wait_ge(h_ready, t + 2)
                groups(h, taken)
                pe.wait_ge(t_act, taken + 2)
                pe.wait_ge(t_dve, taken + 2)
                for k in range(KC):
                    ins = nc.tensor.matmul(rp[:, 0:NR], hT[:, k, :], w_r[:, k, :], start=(k == 0), stop=(k == KC - 1))
                ins.then_inc(r_full, 1)

            pe.wait_ge(w_loaded, 17)
            pe.wait_ge(v_loaded, 144)
            pe.wait_ge(steps, 2)
            mix(0)
            with pe.Fori(1, n_tiles) as t:
                mix(t)
                route(t - 1, t - 1)
            route(n_tiles - 1, n_tiles - 1)

        @block.vector
        def _(dve):
            ch = Chain(dve, steps)

            def take_h(t):
                dve.wait_ge(t_full, 2 * t + 3)
                nc.vector.tensor_copy(hT[:, 4:8, :], tp[1][:, :, :]).then_inc(t_dve, 1)

            def norm(t):
                ch.start(1 + STEPS * t)
                for n in range(2):
                    dve.wait_ge(mix_full, 2 * t + n + 2)
                    ch.step(nc.vector.tensor_tensor(u[:, n * 512:(n + 1) * 512], mp[:, n * 512:(n + 1) * 512],
                                                    bc[:, 0, n * 512:(n + 1) * 512], ALU.mult))
                dve.wait_ge(steps, ch.base + ch.n + 1)
                dve.wait_ge(x_loaded, 16 * (t + 1) + 1)
                ch.link(nc.vector.scalar_tensor_tensor(u[:, :], xt[:, :], ALPHA, u[:, :], ALU.mult, ALU.add))

                def rs(ins):
                    ins.then_inc(mv_ready, 1)
                    dve.wait_ge(mv_ready, t + 2)
                    dve.wait_ge(rstd_ready, t + 2)
                    dve.wait_ge(out_stored, 32 * t + 1)
                    return rstd[:, 0:1]

                norm_steps(nc, dve, ch, u, stats, mv, rs, bc[:, 3, :], bc[:, 4, :], x1[:, :], filler[:, :]).then_inc(x1_ready, 1)
                dve.wait_ge(x1_ready, t + 2)
                ch.link(nc.vector.tensor_tensor(h[:, :], x1[:, :], bc[:, 2, :], ALU.mult))
                assert ch.n == STEPS - 1
                nc.vector.tensor_tensor(h[:, :], h[:, :], bc[:, 1, :], ALU.add).then_inc(h_ready, 1)

            def logits(t):
                dve.wait_ge(r_full, t + 2)
                ch.step(nc.vector.tensor_tensor(LG[:, bass.ds(t + first, 1), :].rearrange("p a n -> p (a n)"), rp[:, 0:NR],
                                                b_r[:, :], ALU.add))

            dve.wait_ge(v_loaded, 144)
            ch.link(nc.vector.tensor_scalar(bc[:, 2, :], bc[:, 2, :], 1.0, None, ALU.add))
            norm(0)
            with dve.Fori(1, n_tiles) as t:
                take_h(t - 1)
                ch.start(STEPS * t)
                logits(t - 1)
                norm(t)
            take_h(n_tiles - 1)
            ch.start(STEPS * n_tiles)
            logits(n_tiles - 1)



def routing(nc, S, C, R, layer):
    t0 = 0 if layer < DEPTH - 1 else CT
    nt = NT - t0
    nb = n_blocks(nt)
    MAXB = nt
    with ExitStack() as cx:
        new_semaphore = cx.enter_context(semaphores(nc))

        def sb(n, shape, dt=F32):
            return cx.enter_context(nc.sbuf_tensor(f"rt_{n}{layer}", shape, dt))

        def sem(n, start=1):
            return new_semaphore(f"rt_{n}{layer}", start)

        T = {k: sb(f"t_{k}", list(C["dram"][k].shape)) for k in ("rev", "edges", "block_no", "upto")}
        h = sb("h", [P, nt, D])
        m = sb("m", [P, nt])
        m1 = sb("m1", [P, nt])
        m2 = sb("m2", [P, nt])
        q = sb("q", [P, nt])
        pstar = sb("pstar", [P, nt])
        e2 = sb("e2", [P, nt])
        r = sb("r", [P, nt, PER])
        ex = sb("ex", [P, nt, NGRP])
        ohg = sb("ohg", [P, nt, NGRP])
        oh = [sb(f"oh{k}", [P, nt, PER]) for k in range(TOPK)]
        sel = sb("sel", [P, nt, NGRP, PER])
        leg = sb("leg", [P, nt, PER])
        E = [sb(f"E{k}", [P, nt, NGRP, PER]) for k in range(TOPK)]
        cnt = sb("cnt", [P, nt, NE])
        big = sb("big", [P, NE * max(NE, nb + 1)])
        nbk = sb("nbk", [P, NE])
        endb = sb("endb", [P, NE])
        start = sb("start", [P, NE])
        total = sb("total", [P, NE])
        pos = sb("pos", [P, nt, NE])
        dest = sb("dest", [P, nt])
        blkf = sb("blkf", [P, nb + 2])
        pp = cx.enter_context(nc.psum_tensor(f"rt_pp{layer}", [P, 512], F32))
        tt = cx.enter_context(nc.psum_tensor(f"rt_tt{layer}", [P, 512], F32))
        h_loaded, step, shifted, exps = sem("h_loaded"), sem("step"), sem("shifted"), sem("exps")
        cnt_ready, prefix_done = sem("cnt_ready"), sem("prefix_done")
        idx_ready, scattered, tables = sem("idx_ready"), sem("scattered", 0), sem("tables")
        block = cx.enter_context(nc.Block())
        LG = R["lg"][:, t0:NT, :]

        @block.sync
        def _(sp):
            for k, tile in T.items():
                sp.dma_start(tile[(slice(None),) * len(tile.shape)], C["dram"][k]).then_inc(tables, 16)
            sp.dma_start(h[:, :, :], S["h_s"][t0 * P:NT * P, :].rearrange("(t p) n -> p t n", p=P)).then_inc(h_loaded, 16)

        @block.scalar
        def _(act):
            act.wait_ge(shifted, 2)
            nc.scalar.activation(ex[:, :, :], ex[:, :, :], ACT.Exp).then_inc(exps, 1)
            act.wait_ge(shifted, 3)
            nc.scalar.activation(e2[:, :], e2[:, :], ACT.Exp).then_inc(exps, 1)

        @block.tensor
        def _(pe):
            pe.wait_ge(cnt_ready, 2)
            for j in range(nt):
                for i in range(j):
                    nc.tensor.matmul(pp[:, j * NE:(j + 1) * NE], C["ones"][:, :], cnt[:, i, :], start=(i == 0), stop=False)
                nc.tensor.matmul(pp[:, j * NE:(j + 1) * NE], C["tri"][:, :], cnt[:, j, :], start=(j == 0), stop=True)
            for i in range(nt):
                ins = nc.tensor.matmul(tt[:, 0:NE], C["ones"][:, :], cnt[:, i, :], start=(i == 0), stop=(i == nt - 1))
            ins.then_inc(prefix_done, 1)

        @block.vector
        def _(dve):
            ch = Chain(dve, step)
            V = nc.vector

            def wide(ap, n):
                return ap.unsqueeze(2).to_broadcast([P, nt, n])

            def first_equal(out, x, mx, rev, n):
                rr = r[:, :, 0:n]
                ch.link(V.tensor_tensor(rr, x, wide(mx, n), ALU.is_equal))
                ch.link(V.tensor_tensor(rr, rr, rev.unsqueeze(1).to_broadcast([P, nt, n]), ALU.mult))
                ch.link(V.tensor_reduce(q[:, :], rr, AX.X, ALU.max))
                ch.link(V.tensor_tensor(out, rr, wide(q[:, :], n), ALU.is_equal))

            lg = LG[:, :, 0:NGRP]
            le = LG[:, :, NGRP:NGRP + NE].rearrange("p t (g x) -> p t g x", g=NGRP)
            dve.wait_ge(tables, 65)
            ch.link(V.tensor_reduce(m[:, :], lg, AX.X, ALU.max))
            V.tensor_tensor(ex[:, :, :], lg, wide(m[:, :], NGRP), ALU.subtract).then_inc(shifted, 1)
            first_equal(ohg[:, :, :], lg, m[:, :], T["rev"][:, PER - NGRP:PER], NGRP)
            ch.link(V.tensor_tensor(sel[:, :, :, :], le, ohg[:, :, :].unsqueeze(3).to_broadcast([P, nt, NGRP, PER]), ALU.mult))
            ch.link(V.tensor_reduce(leg[:, :, :], sel[:, :, :, :].rearrange("p t g x -> p t x g"), AX.X, ALU.add))
            ch.link(V.tensor_reduce(m1[:, :], leg[:, :, :], AX.X, ALU.max))
            first_equal(oh[0][:, :, :], leg[:, :, :], m1[:, :], T["rev"][:, :], PER)
            ch.link(V.scalar_tensor_tensor(leg[:, :, :], oh[0][:, :, :], -BIG, leg[:, :, :], ALU.mult, ALU.add))
            ch.link(V.tensor_reduce(m2[:, :], leg[:, :, :], AX.X, ALU.max))
            V.tensor_tensor(e2[:, :], m2[:, :], m1[:, :], ALU.subtract).then_inc(shifted, 1)
            first_equal(oh[1][:, :, :], leg[:, :, :], m2[:, :], T["rev"][:, :], PER)
            for k in range(TOPK):
                ch.link(V.tensor_tensor(E[k][:, :, :, :], ohg[:, :, :].unsqueeze(3).to_broadcast([P, nt, NGRP, PER]),
                                        oh[k][:, :, :].unsqueeze(2).to_broadcast([P, nt, NGRP, PER]), ALU.mult))
            e_of = [e[:, :, :, :].rearrange("p t g x -> p t (g x)") for e in E]
            V.tensor_tensor(cnt[:, :, :], e_of[0], e_of[1], ALU.add).then_inc(cnt_ready, 1)
            dve.wait_ge(exps, 2)
            ch.link(V.tensor_reduce(q[:, :], ex[:, :, :], AX.X, ALU.add))
            ch.link(V.reciprocal(pstar[:, :], q[:, :]))
            dve.wait_ge(exps, 3)
            ch.link(V.tensor_scalar(q[:, :], e2[:, :], 1.0, None, ALU.add))
            ch.link(V.reciprocal(m[:, :], q[:, :]))
            ch.link(V.tensor_tensor(R["wt"][:, 0, 0:nt], m[:, :], pstar[:, :], ALU.mult))
            ch.link(V.tensor_tensor(R["wt"][:, 1, 0:nt], R["wt"][:, 0, 0:nt], e2[:, :], ALU.mult))
            dve.wait_ge(prefix_done, 2)
            ch.link(V.tensor_copy(total[:, :], tt[:, 0:NE]))
            b3 = big[:, 0:NE * MAXB].rearrange("p (e j) -> p e j", e=NE)
            ch.link(V.tensor_tensor(b3, total[:, :].unsqueeze(2).to_broadcast([P, NE, MAXB]),
                                    T["edges"][:, 0:MAXB].unsqueeze(1).to_broadcast([P, NE, MAXB]), ALU.is_gt))
            ch.link(V.tensor_reduce(nbk[:, :], b3, AX.X, ALU.add))
            b3 = big[:, 0:NE * NE].rearrange("p (e j) -> p e j", e=NE)
            ch.link(V.tensor_tensor(b3, nbk[:, :].unsqueeze(1).to_broadcast([P, NE, NE]), T["upto"][:, :, :], ALU.mult))
            ch.link(V.tensor_reduce(endb[:, :], b3, AX.X, ALU.add))
            ch.link(V.tensor_tensor(start[:, :], endb[:, :], nbk[:, :], ALU.subtract))
            ch.link(V.tensor_scalar(start[:, :], start[:, :], float(P), None, ALU.mult))
            ch.link(V.tensor_tensor(pos[:, :, :], pp[:, 0:nt * NE].rearrange("p (t e) -> p t e", e=NE),
                                    start[:, :].unsqueeze(1).to_broadcast([P, nt, NE]), ALU.add))
            for k in range(TOPK):
                ch.link(V.tensor_tensor(cnt[:, :, :], pos[:, :, :], e_of[k], ALU.mult))
                ch.link(V.tensor_reduce(dest[:, :], cnt[:, :, :], AX.X, ALU.add))
                V.tensor_copy(R["idx"][:, k, 0:nt], dest[:, :]).then_inc(idx_ready, 1)
            b3 = big[:, 0:NE * (nb + 1)].rearrange("p (b e) -> p b e", e=NE)
            ch.link(V.tensor_tensor(b3, endb[:, :].unsqueeze(1).to_broadcast([P, nb + 1, NE]),
                                    T["block_no"][:, 0:nb + 1].unsqueeze(2).to_broadcast([P, nb + 1, NE]), ALU.is_le))
            ch.link(V.tensor_reduce(blkf[:, 0:nb + 1], b3, AX.X, ALU.add))
            ch.link(V.tensor_scalar(blkf[:, 0:nb + 1], blkf[:, 0:nb + 1], float(NE - 1), None, ALU.min))
            ch.link(V.tensor_copy(R["blk"][:, 1:nb + 2], blkf[:, 0:nb + 1]))
            ch.link(V.tensor_copy(R["blk"][:, 0:1], endb[:, NE - 1:NE]))

        @block.gpsimd
        def _(pool):
            pool.wait_ge(h_loaded, 17)
            for k in range(TOPK):
                pool.wait_ge(idx_ready, k + 2)
                for t in range(nt):
                    pool.indirect_dma_start(S["xb"][:, :], bass.IndirectOffsetOnAxis(R["idx"][:, k, t:t + 1], 0),
                                            h[:, t, :], None, bounds_check=S["xb"].shape[0] - 1).then_inc(scattered, 16)
            pool.wait_ge(scattered, 16 * TOPK * nt)



def experts(nc, A, S, C, R, layer):
    nb = n_blocks(NT if layer < DEPTH - 1 else LT)
    turns = (nb + 1) // 2
    FC = FF // P
    with ExitStack() as cx:
        new_semaphore = cx.enter_context(semaphores(nc))

        def sb(n, shape):
            return cx.enter_context(nc.sbuf_tensor(f"ex_{n}{layer}", shape, F32))

        def sem(n, start=1):
            return new_semaphore(f"ex_{n}{layer}", start)

        wg = sb("wg", [P, 2, KC, FF])
        wu = sb("wu", [P, 2, KC, FF])
        wd = sb("wd", [P, 2, FC, D])
        xb = sb("xb", [P, 2, D])
        xT = sb("xT", [P, KC, P])
        sg = sb("sg", [P, FF])
        hm = sb("hm", [P, FF])
        hT = sb("hT", [P, FC, P])
        y = sb("y", [P, 2, D])
        tx = [cx.enter_context(nc.psum_tensor(f"ex_tx{b}_{layer}", [P, 4, P], F32)) for b in range(2)]
        th = cx.enter_context(nc.psum_tensor(f"ex_th{layer}", [P, FC, P], F32))
        gp = cx.enter_context(nc.psum_tensor(f"ex_gp{layer}", [P, FF], F32))
        vp = cx.enter_context(nc.psum_tensor(f"ex_vp{layer}", [P, FF], F32))
        yp = cx.enter_context(nc.psum_tensor(f"ex_yp{layer}", [P, D], F32))
        g_loaded, u_loaded, d_loaded = ([sem(f"{n}_loaded{u}") for u in range(2)] for n in "gud")
        x_loaded = [sem(f"x_loaded{u}", 0) for u in range(2)]
        x_turned, xT_act, xT_dve = sem("x_turned"), sem("xT_act"), sem("xT_dve")
        g_full, u_full, y_full = ([sem(f"{n}_full{u}") for u in range(2)] for n in "guy")
        silu_done, hm_ready, h_turned, hT_ready = sem("silu_done"), sem("hm_ready"), sem("h_turned"), sem("hT_ready")
        y_act, y_dve, y_stored, y_left = sem("y_act"), sem("y_dve"), sem("y_stored", 0), sem("y_left", 2)
        block = cx.enter_context(nc.Block())

        def filled(eng):
            return eng.value_load(R["blk"][0:1, 0:1], min_val=1, max_val=nb)

        @block.sync
        def _(sp):
            n = filled(sp)
            with sp.Fori(0, turns) as i:
                for u in range(2):
                    b = 2 * i + u
                    with sp.If(b < n):
                        e = sp.value_load(R["blk"][0:1, bass.ds(b + 1, 1)], min_val=0, max_val=NE - 1)
                        w = [A[k][layer][bass.ds(e, 1)].rearrange("e (a p) n -> p (e a) n", p=P) for k in ("w_gate", "w_up", "w_down")]
                        sp.wait_ge(g_full[u], i + 1)
                        sp.dma_start(wg[:, u], w[0]).then_inc(g_loaded[u], 16)
                        sp.wait_ge(u_full[u], i + 1)
                        sp.dma_start(wu[:, u], w[1]).then_inc(u_loaded[u], 16)
                        sp.wait_ge(y_full[u], i + 1)
                        sp.dma_start(wd[:, u], w[2]).then_inc(d_loaded[u], 16)

        @block.gpsimd
        def _(pool):
            n = filled(pool)
            rows = S["xb"].rearrange("(b p) n -> b p n", p=P)
            for u in range(2):
                pool.dma_start(xb[:, u, :], rows[u]).then_inc(x_loaded[u], 16)
            pool.wait_ge(x_turned, 3)
            pool.dma_start(xb[:, 0, :], rows[2]).then_inc(x_loaded[0], 16)
            with pool.Fori(0, turns) as i:
                for u in range(2):
                    b = 2 * i + u
                    with pool.If(b < n):
                        pool.wait_ge(y_act, b + 2)
                        pool.wait_ge(y_dve, b + 2)
                        pool.dma_start(rows[bass.ds(b, 1)].rearrange("a p n -> p (a n)"), y[:, u, :]).then_inc(y_stored, 16)
                        pool.wait_ge(x_turned, 2 * b + 5)
                        pool.dma_start(xb[:, 1 - u, :], rows[bass.ds(b + 3, 1)].rearrange("a p n -> p (a n)")).then_inc(x_loaded[1 - u], 16)
                        pool.wait_ge(y_stored, 16 * (b + 1))
                        pool.wait_ge(x_loaded[1 - u], 16 * (i + 2 + u))
                        pool.sem_inc(y_left, 1)

        @block.tensor
        def _(pe):
            def turn_x(u, loads, b):
                pe.wait_ge(x_loaded[u], 16 * loads)
                for k in range(2):
                    pe.wait_ge(xT_act if k == 0 else xT_dve, b + 1)
                    for c in range(4):
                        ins = nc.tensor.transpose(tx[k][:, c, :], xb[:, u, bass.ts(4 * k + c, P)], C["ident"][:, :])
                    ins.then_inc(x_turned, 1)

            n = filled(pe)
            turn_x(0, 1, 0)
            with pe.Fori(0, turns) as i:
                for u in range(2):
                    b = 2 * i + u
                    with pe.If(b < n):
                        pe.wait_ge(xT_act, b + 2)
                        pe.wait_ge(xT_dve, b + 2)
                        pe.wait_ge(g_loaded[u], 16 * (i + 1) + 1)
                        pe.wait_ge(silu_done, b + 1)
                        for k in range(KC):
                            ins = nc.tensor.matmul(gp[:, :], xT[:, k, :], wg[:, u, k, :], start=(k == 0), stop=(k == KC - 1))
                        ins.then_inc(g_full[u], 1)
                        pe.wait_ge(u_loaded[u], 16 * (i + 1) + 1)
                        pe.wait_ge(hm_ready, b + 1)
                        for k in range(KC):
                            ins = nc.tensor.matmul(vp[:, :], xT[:, k, :], wu[:, u, k, :], start=(k == 0), stop=(k == KC - 1))
                        ins.then_inc(u_full[u], 1)
                        turn_x(1 - u, i + 1 + u, b + 1)
                        pe.wait_ge(hm_ready, b + 2)
                        pe.wait_ge(hT_ready, b + 1)
                        for c in range(FC):
                            ins = nc.tensor.transpose(th[:, c, :], hm[:, bass.ts(c, P)], C["ident"][:, :])
                        ins.then_inc(h_turned, 1)
                        pe.wait_ge(hT_ready, b + 2)
                        pe.wait_ge(d_loaded[u], 16 * (i + 1) + 1)
                        pe.wait_ge(y_act, b + 1)
                        pe.wait_ge(y_dve, b + 1)
                        for m in range(2):
                            for c in range(FC):
                                ins = nc.tensor.matmul(yp[:, m * 512:(m + 1) * 512], hT[:, c, :], wd[:, u, c, m * 512:(m + 1) * 512],
                                                       start=(c == 0), stop=(c == FC - 1))
                        ins.then_inc(y_full[u], 1)

        @block.scalar
        def _(act):
            def take_x(b):
                act.wait_ge(x_turned, 2 * b + 2)
                nc.scalar.activation(xT[:, 0:4, :], tx[0][:, :, :], ACT.Copy).then_inc(xT_act, 1)

            n = filled(act)
            take_x(0)
            with act.Fori(0, turns) as i:
                for u in range(2):
                    b = 2 * i + u
                    with act.If(b < n):
                        act.wait_ge(g_full[u], i + 2)
                        act.wait_ge(hm_ready, b + 1)
                        nc.scalar.activation(sg[:, :], gp[:, :], ACT.Silu).then_inc(silu_done, 1)
                        take_x(b + 1)
                        act.wait_ge(y_full[u], i + 2)
                        act.wait_ge(y_left, b + 1)
                        nc.scalar.activation(y[:, u, 0:512], yp[:, 0:512], ACT.Copy).then_inc(y_act, 1)

        @block.vector
        def _(dve):
            def take_x(b):
                dve.wait_ge(x_turned, 2 * b + 3)
                nc.vector.tensor_copy(xT[:, 4:8, :], tx[1][:, :, :]).then_inc(xT_dve, 1)

            n = filled(dve)
            take_x(0)
            with dve.Fori(0, turns) as i:
                for u in range(2):
                    b = 2 * i + u
                    with dve.If(b < n):
                        dve.wait_ge(u_full[u], i + 2)
                        dve.wait_ge(silu_done, b + 2)
                        dve.wait_ge(h_turned, b + 1)
                        nc.vector.tensor_tensor(hm[:, :], sg[:, :], vp[:, :], ALU.mult).then_inc(hm_ready, 1)
                        take_x(b + 1)
                        dve.wait_ge(h_turned, b + 2)
                        nc.vector.tensor_copy(hT[:, :, :], th[:, :, :]).then_inc(hT_ready, 1)
                        dve.wait_ge(y_full[u], i + 2)
                        dve.wait_ge(y_left, b + 1)
                        nc.vector.tensor_copy(y[:, u, 512:D], yp[:, 512:D]).then_inc(y_dve, 1)



def combine(nc, A, S, C, R, layer, out):
    last = layer == DEPTH - 1
    t0 = CT if last else 0
    nt = NT - t0
    with ExitStack() as cx:
        new_semaphore = cx.enter_context(semaphores(nc))

        def sb(n, shape):
            return cx.enter_context(nc.sbuf_tensor(f"cb_{n}{layer}", shape, F32))

        def sem(n, start=1):
            return new_semaphore(f"cb_{n}{layer}", start)

        y = [sb(f"y{k}", [P, nt, D]) for k in range(TOPK)]
        bc = sb("bc", [P, 4, D])
        xt = sb("xt", [P, D])
        u = sb("u", [P, D])
        x2 = sb("x2", [P, D])
        stats = sb("stats", [P, 2, 6])
        mv = sb("mv", [P, 2])
        veps = sb("veps", [P, 1])
        rstd = sb("rstd", [P, 1])
        filler = sb("filler", [P, 1])
        gathered, w_loaded, x_loaded = [sem(f"gathered{t}", 0) for t in range(nt)], sem("w_loaded"), sem("x_loaded")
        steps, mv_ready, eps_done, rstd_ready = sem("steps"), sem("mv_ready"), sem("eps_done"), sem("rstd_ready")
        x_used, x2_ready, out_stored = sem("x_used"), sem("x2_ready"), sem("out_stored")
        block = cx.enter_context(nc.Block())
        STEPS = 7

        @block.gpsimd
        def _(pool):
            for t in range(nt):
                for k in range(TOPK):
                    pool.indirect_dma_start(y[k][:, t, :], None, S["xb"][:, :],
                                            bass.IndirectOffsetOnAxis(R["idx"][:, k, t:t + 1], 0),
                                            bounds_check=S["xb"].shape[0] - 1).then_inc(gathered[t], 16)
            for t in range(nt):
                pool_rstd(nc, pool, C, mv, veps, rstd, mv_ready, eps_done, rstd_ready, t)

        @block.sync
        def _(sp):
            c0 = layer * 6 * D + 5 * D
            sp.dma_start(bc[:, 0, :], S["ada"][0, c0:c0 + D].partition_broadcast(P)).then_inc(w_loaded, 16)
            sp.dma_start(bc[:, 1, :], S["ada"][1, c0:c0 + D].partition_broadcast(P)).then_inc(w_loaded, 16)
            sp.dma_start(bc[:, 2, :], A["ln2_g"][layer].partition_broadcast(P)).then_inc(w_loaded, 16)
            sp.dma_start(bc[:, 3, :], A["ln2_b"][layer].partition_broadcast(P)).then_inc(w_loaded, 16)
            xs = S["x_s"].rearrange("(t p) n -> t p n", p=P)
            dst = (out[0] if last else S["x_s"]).rearrange("(t p) n -> t p n", p=P)
            with sp.Fori(0, nt) as t:
                sp.wait_ge(x_used, t + 1)
                sp.dma_start(xt[:, :], xs[bass.ds(t + t0, 1)].rearrange("a p n -> p (a n)")).then_inc(x_loaded, 16)
                sp.wait_ge(x2_ready, t + 2)
                sp.dma_start(dst[bass.ds(t, 1)].rearrange("a p n -> p (a n)"), x2[:, :]).then_inc(out_stored, 16)
            sp.wait_ge(out_stored, 16 * nt + 1)

        @block.vector
        def _(dve):
            ch = Chain(dve, steps)
            dve.wait_ge(w_loaded, 65)
            for gate, first, n in ((0, 0, CT), (1, CT, LT)):
                if last and gate == 0:
                    continue
                done = 0 if last else first
                for i in range(n):
                    t = i + done
                    dve.wait_ge(gathered[t], 16 * TOPK)
                    ch.start((i + done) * STEPS)
                    dve.wait_ge(x2_ready, t + 1)
                    w = [R["wt"][:, k, bass.ds(t, 1)] for k in range(TOPK)]
                    ya, yc = (y[k][:, bass.ds(t, 1), :].rearrange("p a n -> p (a n)") for k in range(TOPK))
                    ch.link(nc.vector.tensor_scalar(u[:, :], ya, w[0], None, ALU.mult))
                    ch.link(nc.vector.scalar_tensor_tensor(u[:, :], yc, w[1], u[:, :], ALU.mult, ALU.add))
                    ch.link(nc.vector.tensor_tensor(u[:, :], u[:, :], bc[:, gate, :], ALU.mult))
                    dve.wait_ge(x_loaded, 16 * (t + 1) + 1)
                    nc.vector.scalar_tensor_tensor(u[:, :], xt[:, :], ALPHA, u[:, :], ALU.mult, ALU.add).then_inc(x_used, 1)
                    dve.wait_ge(x_used, t + 2)

                    def rs(ins):
                        ins.then_inc(mv_ready, 1)
                        dve.wait_ge(mv_ready, t + 2)
                        dve.wait_ge(rstd_ready, t + 2)
                        dve.wait_ge(out_stored, 16 * t + 1)
                        return rstd[:, 0:1]

                    norm_steps(nc, dve, ch, u, stats, mv, rs, bc[:, 2, :], bc[:, 3, :], x2[:, :], filler[:, :]).then_inc(x2_ready, 1)
                    assert ch.n == STEPS



CONSTS = ("ident", "tri", "ones", "mhalf", "eps")


def backbone(nc, A, consts, out, stop=None):
    S = {}

    def dram(name, shape):
        S[name] = nc.dram_tensor(name, shape, F32, kind="Internal").ap()

    dram("x_s", [NT * P, D])
    dram("h_s", [NT * P, D])
    dram("o_s", [NT, P, KC, P])
    dram("ada", [2, DEPTH * 6 * D])
    dram("q_mla", [NT, 2, QK, H_MLA, P])
    dram("q_gqa", [NT, P, H_GQA, P])
    dram("k_mla", [2, QK, H_MLA, NT * P])
    dram("k_gqa", [P, 2 * H_KV, NT * P])
    dram("v_s", [NT * P, (H_MLA + H_KV) * VD])
    dram("xb", [(NBP + 3) * P, D])
    with ExitStack() as cx:
        C = {k: cx.enter_context(nc.sbuf_tensor(f"c_{k}", list(consts[k].shape), F32)) for k in CONSTS}
        C["dram"] = consts
        C["xb_zeroed"] = cx.enter_context(nc.semaphore("xb_zeroed"))
        R = {"lg": cx.enter_context(nc.sbuf_tensor("logits", [P, NT, NGRP + NE], F32)),
             "wt": cx.enter_context(nc.sbuf_tensor("weights", [P, TOPK, NT], F32)),
             "idx": cx.enter_context(nc.sbuf_tensor("slots", [P, TOPK, NT], I32)),
             "blk": cx.enter_context(nc.sbuf_tensor("blocks", [P, NB + 3], I32))}
        loaded = cx.enter_context(nc.semaphore("consts_loaded"))
        with nc.Block() as block:
            @block.sync
            def _(sp):
                for k in CONSTS:
                    n = len(consts[k].shape)
                    at = (slice(None),) * n
                    sp.dma_start(C[k][at], consts[k]).then_inc(loaded, 16)
                sp.wait_ge(loaded, 16 * len(CONSTS))
        modulation(nc, A, S)
        if stop == "ada":
            return S
        for layer in range(DEPTH):
            with nc.sbuf_tensor(f"zeros{layer}", [P, D if layer == 0 else 8], F32) as zeros:
                C["zeros"] = zeros
                projections(nc, A, S, C, layer)
            if stop == "proj":
                return S
            with ExitStack() as kx:
                new_semaphore = kx.enter_context(semaphores(nc))
                KV = {"k_mla": [kx.enter_context(nc.sbuf_tensor(f"k_mla{n}_{layer}", [QK, H_MLA, NT * P], F32R)) for n in range(2)],
                      "k_gqa": kx.enter_context(nc.sbuf_tensor(f"k_gqa{layer}", [P, 2 * H_KV, NT * P], F32R)),
                      "v": kx.enter_context(nc.sbuf_tensor(f"v_all{layer}", [P, NT, (H_MLA + H_KV) * VD], F32)),
                      "k_loaded": [new_semaphore(f"k_loaded{j}_{layer}") for j in range(H_MLA // 2 + 1)],
                      "v_loaded": new_semaphore(f"v_loaded{layer}"), "fresh": True}
                if layer < DEPTH - 1:
                    attention(nc, S, C, KV, layer, (0, CT), CT, "ctx")
                    KV["fresh"] = False
                attention(nc, S, C, KV, layer, (CT, NT), NT, "lat")
            if stop == "attn":
                return S
            if layer < DEPTH - 1:
                mix_and_route(nc, A, S, C, R["lg"], layer, 0)
            mix_and_route(nc, A, S, C, R["lg"], layer, 1)
            if stop == "mix":
                return S
            routing(nc, S, C, R, layer)
            if stop == "route":
                return S
            experts(nc, A, S, C, R, layer)
            combine(nc, A, S, C, R, layer, out)
            if stop == "layer0":
                return S
    return S


_INS = ["x", "c", "ctx", "c_ctx", "w_ada", "b_ada", "w_in", "g_q_a", "w_q_b", "g_kv_a", "w_kv_b", "g_gqa_q", "g_gqa_k",
        "w_o", "ln1_g", "ln1_b", "w_router_grp", "b_router_grp", "w_router_exp", "b_router_exp",
        "w_gate", "w_up", "w_down", "ln2_g", "ln2_b"]


def constants():
    f = np.float32
    i = np.arange(P)
    c = {"ident": np.eye(P, dtype=f), "tri": (i[:, None] < i[None, :]).astype(f), "ones": np.ones((P, P), f),
         "mhalf": np.full((P, 16), -0.5, f)}
    c["eps"] = np.full((P, 16), RMS_EPS, f)
    c["eps"][:, 15] = LN_EPS

    def all_rows(v):
        return np.ascontiguousarray(np.broadcast_to(np.asarray(v, f), (P,) + np.shape(v)))
    c["rev"] = all_rows(np.arange(PER, 0, -1))
    c["edges"] = all_rows(P * np.arange(NT))
    c["block_no"] = all_rows(np.arange(NB + 2))
    e = np.arange(NE)
    c["upto"] = all_rows(e[:, None] >= e[None, :])
    pos = np.arange(SEQ)
    rc = np.stack([pos // GRID_W, pos % GRID_W]).astype(f)
    for name, dim in (("rope_mla", ROPE), ("rope_gqa", HD)):
        half = dim // 2
        inv = (f(ROPE_BASE) ** (-(np.arange(0, half, 2, dtype=f) / f(half)))).astype(f)
        ang = (rc[:, :, None] * inv).astype(f).astype(np.float64)
        cos, sin = np.cos(ang).astype(f), np.sin(ang).astype(f)
        t = np.zeros((NT, P, 2, 2, 2, half // 2), f)
        t[:, :, 0] = 1.0
        for p in range(2):
            for h in range(2):
                t[CT:, :, 0, p, h] = cos[p].reshape(LT, P, -1)
                t[CT:, :, 1, p, h] = sin[p].reshape(LT, P, -1) * (-1 if h == 0 else 1)
        c[name] = np.ascontiguousarray(t.transpose(1, 0, 2, 3, 4, 5).reshape(P, NT, 2, dim))
    return c


def kernel(**inputs):
    import concourse.bacc as _bacc
    from concourse.bass_utils import run_bass_kernel_spmd as _run

    nc = _bacc.Bacc("TRN2", target_bir_lowering=False, num_devices=1)
    arrays, A, consts = {}, {}, {}
    for name in _INS:
        a = np.ascontiguousarray(inputs[name])
        arrays[f"in_{name}"] = a
        A[name] = nc.dram_tensor(f"in_{name}", a.shape, mybir.dt.from_np(a.dtype), kind="ExternalInput").ap()
    for name, a in constants().items():
        arrays[f"const_{name}"] = a
        consts[name] = nc.dram_tensor(f"const_{name}", a.shape, F32, kind="ExternalInput").ap()
    out = nc.dram_tensor("out_0", (1, SEQ, D), F32, kind="ExternalOutput").ap()
    backbone(nc, A, consts, out)
    r = _run(nc, [arrays], core_ids=[0])
    return r.results[0]["out_0"]
```
